# Optimizing a Trainium2 kernel written in Bass

```python
import jax, jax.numpy as jnp
from jax import lax
import numpy as np

D_MODEL = 1024
BATCH = 1
SEQ = 512
DEPTH = 1
DEC_BATCH = 8
DEC_SEQ = 8
PAST_LEN = 4096
PAGE_SIZE = 128

MIX_WIDTH = D_MODEL
POOL_CH = MIX_WIDTH // 2
CONV_CH = MIX_WIDTH - POOL_CH
POOL_WINDOWS = (2, 4, 8, 16)
N_POOL_GROUPS = len(POOL_WINDOWS)
POOL_GROUP = POOL_CH // N_POOL_GROUPS
POOL_BUF = max(POOL_WINDOWS) - 1
CONV_TAPS = 31
CONV_BUF = CONV_TAPS - 1
IN_COLS = POOL_CH + 2 * CONV_CH
N_EXPERTS = 32
TOP_K = 4
D_FF = D_MODEL
SWIGLU_LIMIT = 7.0
SWIGLU_ALPHA = 1.702
MOE_BLOCK = 128
RMS_EPS = 1e-5
LN_EPS = 1e-5

kernel_name = "hymba_pool_conformer_moe_step"

def rmsnorm(x, g):
    xf = x.astype(jnp.float32)
    y = xf * lax.rsqrt(jnp.mean(xf * xf, axis=-1, keepdims=True) + RMS_EPS)
    return (y * g.astype(jnp.float32)).astype(x.dtype)

def pool_mix(u, buf, pos0, pool_w, pool_scale):
    B, T, _ = u.shape
    cat = jnp.concatenate([buf.astype(u.dtype), u], axis=1)
    cs = jnp.cumsum(cat.astype(jnp.float32), axis=1)
    cs = jnp.pad(cs, ((0, 0), (1, 0), (0, 0)))
    pos = pos0 + jnp.arange(T, dtype=jnp.int32)
    means = []
    for g, w in enumerate(POOL_WINDOWS):
        c0, c1 = g * POOL_GROUP, (g + 1) * POOL_GROUP
        hi = cs[:, POOL_BUF + 1:POOL_BUF + 1 + T, c0:c1]
        lo = cs[:, POOL_BUF + 1 - w:POOL_BUF + 1 - w + T, c0:c1]
        cnt = jnp.minimum(w, pos + 1).astype(jnp.float32)
        means.append((hi - lo) / cnt[None, :, None])
    mean = jnp.stack(means, axis=2)
    z = mean - u.reshape(B, T, N_POOL_GROUPS, POOL_GROUP).astype(jnp.float32)
    y = jnp.einsum('btgc,gcd->btgd', z.astype(u.dtype), pool_w).reshape(B, T, POOL_CH)
    return y * pool_scale, cat[:, -POOL_BUF:]

def conv_mix(v, buf, conv_w, conv_b, ln_g, ln_b):
    a, gt = v[..., :CONV_CH], v[..., CONV_CH:]
    glu = a * jax.nn.sigmoid(gt)
    cat = jnp.concatenate([buf.astype(glu.dtype), glu], axis=1)
    d = lax.conv_general_dilated(cat, conv_w[:, None, :].astype(cat.dtype), window_strides=(1,),
                                 padding='VALID', dimension_numbers=('NWC', 'WIO', 'NWC'),
                                 feature_group_count=CONV_CH) + conv_b
    df = d.astype(jnp.float32)
    mu = jnp.mean(df, axis=-1, keepdims=True)
    var = jnp.mean(jnp.square(df - mu), axis=-1, keepdims=True)
    n = ((df - mu) * lax.rsqrt(var + LN_EPS) * ln_g.astype(jnp.float32) + ln_b.astype(jnp.float32)).astype(d.dtype)
    return jax.nn.silu(n), cat[:, -CONV_BUF:]

def moe(x2, w_router, b_router, w_gate_up, b_gate_up, w_down, b_down):
    N, D = x2.shape
    logits = (x2 @ w_router + b_router).astype(jnp.float32)
    top_val, top_idx = lax.top_k(logits, TOP_K)
    gate = jax.nn.softmax(top_val, axis=-1)
    M = N * TOP_K
    flat_e = top_idx.reshape(-1).astype(jnp.int32)
    flat_tok = jnp.repeat(jnp.arange(N, dtype=jnp.int32), TOP_K)
    flat_w = gate.reshape(-1)
    order = jnp.argsort(flat_e)
    sorted_e = flat_e[order]
    counts = jnp.bincount(flat_e, length=N_EXPERTS).astype(jnp.int32)
    padded = (counts + MOE_BLOCK - 1) // MOE_BLOCK * MOE_BLOCK
    offs = jnp.cumsum(counts) - counts
    pad_end = jnp.cumsum(padded)
    pad_offs = pad_end - padded
    dest = pad_offs[sorted_e] + (jnp.arange(M, dtype=jnp.int32) - offs[sorted_e])
    n_blocks = -(-M // MOE_BLOCK) + N_EXPERTS
    P = n_blocks * MOE_BLOCK
    row_tok = jnp.full((P,), N, jnp.int32).at[dest].set(flat_tok[order])
    row_w = jnp.zeros((P,), jnp.float32).at[dest].set(flat_w[order])
    block_start = jnp.arange(n_blocks, dtype=jnp.int32) * MOE_BLOCK
    block_e = jnp.minimum(jnp.searchsorted(pad_end, block_start, side='right'), N_EXPERTS - 1).astype(jnp.int32)
    x_pad = jnp.concatenate([x2, jnp.zeros((1, D), x2.dtype)], axis=0)
    xb = x_pad[row_tok].reshape(n_blocks, MOE_BLOCK, D)

    def expert_block(args):
        xblk, e = args
        gu = xblk @ w_gate_up[e] + b_gate_up[e]
        g, up = gu[..., :D_FF], gu[..., D_FF:]
        g = jnp.minimum(g, SWIGLU_LIMIT)
        up = jnp.clip(up, -SWIGLU_LIMIT, SWIGLU_LIMIT)
        hdn = (up + 1.0) * (g * jax.nn.sigmoid(SWIGLU_ALPHA * g))
        return hdn @ w_down[e] + b_down[e]

    yb = lax.map(expert_block, (xb, block_e)).reshape(P, D)
    yb = yb * row_w[:, None].astype(yb.dtype)
    return jax.ops.segment_sum(yb, row_tok, num_segments=N + 1)[:N]

def trunk(x, pool_buf, conv_buf, pos0, g_mix, w_in, pool_w, pool_scale, conv_w, conv_b,
          conv_ln_g, conv_ln_b, w_out, g_moe, w_router, b_router, w_gate_up, b_gate_up,
          w_down, b_down, g_final):
    B, T, D = x.shape
    new_pool, new_conv = [], []
    for l in range(DEPTH):
        xn = rmsnorm(x, g_mix[l])
        proj = xn @ w_in[l]
        y_pool, nb_pool = pool_mix(proj[..., :POOL_CH], pool_buf[l], pos0, pool_w[l], pool_scale[l])
        y_conv, nb_conv = conv_mix(proj[..., POOL_CH:], conv_buf[l], conv_w[l], conv_b[l],
                                   conv_ln_g[l], conv_ln_b[l])
        h = x + jnp.concatenate([y_pool, y_conv], axis=-1) @ w_out[l]
        hn = rmsnorm(h, g_moe[l]).reshape(B * T, D)
        x = h + moe(hn, w_router[l], b_router[l], w_gate_up[l], b_gate_up[l],
                    w_down[l], b_down[l]).reshape(B, T, D)
        new_pool.append(nb_pool)
        new_conv.append(nb_conv)
    return rmsnorm(x, g_final), jnp.stack(new_pool), jnp.stack(new_conv)

def setup_inputs(seed: int = 0) -> dict:
    key = jax.random.key(seed)
    ks = jax.random.split(key, 24)
    f = jnp.float32
    nrm = lambda k, shape, s: jax.random.normal(k, shape, f) * s
    return {
        "x_prompt": nrm(ks[0], (BATCH, SEQ, D_MODEL), 1.0),
        "x_sample": nrm(ks[1], (DEC_BATCH, DEC_SEQ, D_MODEL), 1.0),
        "state_pool": nrm(ks[2], (DEPTH, DEC_BATCH, POOL_BUF, POOL_CH), 1.0),
        "state_conv": nrm(ks[3], (DEPTH, DEC_BATCH, CONV_BUF, CONV_CH), 0.5),
        "g_mix": 1.0 + nrm(ks[4], (DEPTH, D_MODEL), 0.1),
        "w_in": nrm(ks[5], (DEPTH, D_MODEL, IN_COLS), D_MODEL ** -0.5),
        "pool_w": nrm(ks[6], (DEPTH, N_POOL_GROUPS, POOL_GROUP, POOL_GROUP), POOL_GROUP ** -0.5),
        "pool_scale": 1.0 + nrm(ks[7], (DEPTH, POOL_CH), 0.1),
        "conv_w": nrm(ks[8], (DEPTH, CONV_TAPS, CONV_CH), CONV_TAPS ** -0.5),
        "conv_b": nrm(ks[9], (DEPTH, CONV_CH), 0.01),
        "conv_ln_g": 1.0 + nrm(ks[10], (DEPTH, CONV_CH), 0.1),
        "conv_ln_b": nrm(ks[11], (DEPTH, CONV_CH), 0.01),
        "w_out": nrm(ks[12], (DEPTH, MIX_WIDTH, D_MODEL), MIX_WIDTH ** -0.5),
        "g_moe": 1.0 + nrm(ks[13], (DEPTH, D_MODEL), 0.1),
        "w_router": nrm(ks[14], (DEPTH, D_MODEL, N_EXPERTS), D_MODEL ** -0.5),
        "b_router": nrm(ks[15], (DEPTH, N_EXPERTS), 0.01),
        "w_gate_up": nrm(ks[16], (DEPTH, N_EXPERTS, D_MODEL, 2 * D_FF), D_MODEL ** -0.5),
        "b_gate_up": nrm(ks[17], (DEPTH, N_EXPERTS, 2 * D_FF), 0.01),
        "w_down": nrm(ks[18], (DEPTH, N_EXPERTS, D_FF, D_MODEL), D_FF ** -0.5),
        "b_down": nrm(ks[19], (DEPTH, N_EXPERTS, D_MODEL), 0.01),
        "g_final": 1.0 + nrm(ks[20], (D_MODEL,), 0.1),
    }

def reference(x_prompt, x_sample, state_pool, state_conv, g_mix, w_in, pool_w, pool_scale,
              conv_w, conv_b, conv_ln_g, conv_ln_b, w_out, g_moe, w_router, b_router,
              w_gate_up, b_gate_up, w_down, b_down, g_final):
    B = x_prompt.shape[0]
    zero_pool = jnp.zeros((DEPTH, B, POOL_BUF, POOL_CH), x_prompt.dtype)
    zero_conv = jnp.zeros((DEPTH, B, CONV_BUF, CONV_CH), x_prompt.dtype)
    y_prompt, pool_p, conv_p = trunk(x_prompt, zero_pool, zero_conv, 0, g_mix, w_in, pool_w,
                                     pool_scale, conv_w, conv_b, conv_ln_g, conv_ln_b, w_out,
                                     g_moe, w_router, b_router, w_gate_up, b_gate_up, w_down,
                                     b_down, g_final)
    y_sample, pool_s, conv_s = trunk(x_sample, state_pool, state_conv, PAST_LEN, g_mix, w_in,
                                     pool_w, pool_scale, conv_w, conv_b, conv_ln_g, conv_ln_b,
                                     w_out, g_moe, w_router, b_router, w_gate_up, b_gate_up,
                                     w_down, b_down, g_final)
    return (y_prompt, y_sample, pool_p, conv_p, pool_s, conv_s)


_drawn_inputs = setup_inputs


def setup_inputs(seed=0):
    import zlib

    import numpy as np

    out = dict(_drawn_inputs(seed))
    spreads = {}
    factors = {'conv_ln_b': 2.997, 'b_gate_up': 8.0, 'b_down': 8.0, 'b_router': 2.718}
    for name, (base, spread) in spreads.items():
        noise = np.random.default_rng([zlib.crc32(name.encode()), seed]).standard_normal(out[name].shape)
        drawn = base * np.exp(spread * noise) if base else spread * noise
        out[name] = __import__('jax').numpy.asarray(drawn.astype(out[name].dtype))
    for name, factor in factors.items():
        out[name] = (out[name] * factor).astype(out[name].dtype)
    return out
```

```python
from contextlib import ExitStack

import concourse.bass as bass
from concourse import mybir

P = 128
F32 = mybir.dt.float32
F16 = mybir.dt.float16
I32 = mybir.dt.int32
U32 = mybir.dt.uint32
ALU = mybir.AluOpType
ACT = mybir.ActivationFunctionType
AX = mybir.AxisListType

WINDOWS = (2, 4, 8, 16)
TOP_K = 4
RMS_EPS = 1e-5
LN_EPS = 1e-5
NO_ROW = 1 << 16
LIMIT = 7.0
ALPHA = 1.702
RING = 8
SLOT = 2048


def hybrid_moe_step(nc, x_prompt, x_sample, state_pool, state_conv, g_mix, w_in, pool_w, pool_scale,
                    conv_w, conv_b, conv_ln_g, conv_ln_b, w_out, g_moe, w_router, b_router,
                    w_gate_up, b_gate_up, w_down, b_down, g_final,
                    y_prompt, y_sample, pool_prompt, conv_prompt, pool_sample, conv_sample,
                    normed_dram, rows_dram):
    _, SEQ, D = x_prompt.shape
    NB, NT, _ = x_sample.shape
    NS = NB * NT
    T = SEQ + NS
    CH = pool_scale.shape[1]
    G = CH // P
    TAPS = conv_w.shape[1]
    PB, CB = state_pool.shape[2], state_conv.shape[2]
    E = w_router.shape[2]
    K = D // P
    FF = w_down.shape[2]
    KF = FF // P
    rows = [P] * (SEQ // P) + [NS]
    J = len(rows)
    MAX_OVER = TOP_K * T // P
    COLS = E + MAX_OVER + 2
    GU_CHUNKS, DN_CHUNKS = K, KF // 2
    IN_CHUNKS, OUT_CHUNKS = 6, K // 2
    MIX_CHUNKS = IN_CHUNKS + OUT_CHUNKS
    assert D == 1024 and CH == 512 and FF == D and SEQ == 512 and NS == 64
    assert (2 * (GU_CHUNKS + DN_CHUNKS)) % RING == 0
    HALF = 4

    with ExitStack() as ctx:
        def sb(name, shape, dt=F32):
            return ctx.enter_context(nc.sbuf_tensor(name, shape, dt))

        def sem(name):
            return ctx.enter_context(nc.semaphore(name))

        ring = sb("ring", [P, RING, SLOT])
        h = sb("h", [P, J, D])
        row_buf = [sb(f"row_buf{i}", [P, D]) for i in range(2)]
        xT = [sb(f"xT{i}", [P, K, P]) for i in range(2)]
        mixT = sb("mixT", [P, K, T])
        xnT = mixT
        yT = mixT
        u_p = sb("u_p", [P, G, PB + SEQ])
        u_s = sb("u_s", [P, G, NB, PB + NT])
        glu_p = sb("glu_p", [P, G, CB + SEQ])
        glu_s = sb("glu_s", [P, G, NB, CB + NT])
        shared = sb("shared", [P, 2, G * T])
        conv = shared[:, 0, :].rearrange("p (c t) -> p c t", c=G)
        z = shared[:, 1, :].rearrange("p (c t) -> p c t", c=G)
        flat = shared[:, :, :].rearrange("p a n -> p (a n)")
        gate_s, up_s, sig_s = (flat[:, n * FF:(n + 1) * FF] for n in range(3))
        sig_p = [sb(f"sig_p{i}", [P, T]) for i in range(2)]
        win_p = [sb(f"win_p{i}", [P, PB + SEQ]) for i in range(2)]
        win_s = [sb(f"win_s{i}", [P, NB, PB + NT]) for i in range(2)]
        newest = [xT[i][:, 0:2, :].rearrange("p k t -> p (k t)").rearrange("p (c t) -> p c t", c=G) for i in range(2)]
        spare = mixT[:, :, :].rearrange("p k t -> p (k t)")
        hT = spare[:, 0:FF].rearrange("p (k t) -> p k t", k=KF)
        gfin = spare[:, FF:FF + D]
        oh = spare[:, 2048:2048 + J * TOP_K * E].rearrange("p (j k e) -> p j k e", j=J, k=TOP_K)
        inA = spare[:, 3840:3840 + TOP_K * P // 2].bitcast(F16).rearrange("p (k s) -> p k s", k=TOP_K)
        inB = spare[:, 4096:4096 + TOP_K * COLS].bitcast(F16).rearrange("p (k a n) -> p k a n", k=TOP_K, a=2)
        cmp = spare[:, 3072:3072 + (COLS - E) * E].rearrange("p (n e) -> p n e", e=E)
        y_sb = [sb(f"y_sb{i}", [P, D]) for i in range(2)]
        bias = sb("bias", [E, 2 * FF + D])
        vec_rows = sb("vec_rows", [32, P])
        cw_rows = y_sb[0][0:TAPS, CH:2 * CH]
        sp_rows = y_sb[0][0:NB * PB, 0:CH]
        sc_rows = y_sb[1][0:NB // 2 * CB, :].rearrange("p (a n) -> p a n", a=2)
        tails = [y_sb[0][:, 512:1024], sb("tail1", [64, CH])]
        poolw = sb("poolw", [P, G, P])
        router = sb("router", [P, K, E])
        br = sb("br", [P, E])
        vecT = sb("vecT", [P, 32])
        cwT = sb("cwT", [P, G, TAPS])
        ident = sb("ident", [P, P])
        before = sb("before", [P, P], F16)
        ones = sb("ones", [P, P], F16)
        iota_s = sb("iota_s", [P, P])
        tokid = sb("tokid", [P, J])
        base1 = sb("base1", [P, E])
        part = sb("part", [P, 1])
        inv = sb("inv", [P, PB])
        eps = sb("eps", [P, 1])
        ss = sb("ss", [P, 4, J])
        mv = sb("mv", [P, J, 2])
        st = sb("st", [P, 6])
        lnr = sb("lnr", [P, 2, J])
        fix = sb("fix", [P, PB])
        L = sb("L", [P, J, E])
        v8 = sb("v8", [P, J, 8])
        i8 = sb("i8", [P, J, 8], U32)
        idxf = sb("idxf", [P, J, TOP_K])
        mask = sb("mask", [P, J, E], F16)
        gates = sb("gates", [P, J, TOP_K])
        gsum = sb("gsum", [P, 2, J])
        over = sb("over", [P, 5, E])
        dest = sb("dest", [P, J, E])
        dest4 = sb("dest4", [P, J, TOP_K])
        desti = sb("desti", [P, 3, J, TOP_K], I32)
        dmod = sb("dmod", [P, 2, J, TOP_K])
        nth = sb("nth", [P, TOP_K])
        none = sb("none", [P, COLS])
        tok_f = sb("tok_f", [P, COLS])
        blk_e = sb("blk_e", [P, COLS])
        blk_i = sb("blk_i", [1, COLS], I32)
        selm = sb("selm", [E, COLS])
        slot_tok = sb("slot_tok", [P, COLS], U32)
        slot_row = sb("slot_row", [P, COLS], U32)
        idx_cur = [sb(f"idx_cur{i}", [P, 1], U32) for i in range(2)]
        row_cur = [sb(f"row_cur{i}", [P, 1], U32) for i in range(2)]
        sel_cur = [sb(f"sel_cur{i}", [E, P]) for i in range(2)]
        nit_f = sb("nit_f", [P, 2])
        nit_i = sb("nit_i", [P, 2], I32)
        ps = ctx.enter_context(nc.psum_tensor("ps", [P, 8, 512], F32))
        psg = ps[:, 4:6, :].rearrange("p b n -> p (b n)")
        psu = ps[:, 6:8, :].rearrange("p b n -> p (b n)")
        psd = ps[:, 2:4, :].rearrange("p b n -> p (b n)")

        gmixT, gmoeT = vecT[:, 0:8], vecT[:, 8:16]
        pscale, convb, lng, lnb = (vecT[:, 16 + 4 * n:20 + 4 * n] for n in range(4))

        s_cst = sem("s_cst")
        s_pad = sem("s_pad")
        s_vec = sem("s_vec")
        s_x = [sem(f"s_x{j}") for j in range(J)]
        s_ring = [sem(f"s_ring{n}") for n in range(RING)]
        s_used = sem("s_used")
        s_poolw, s_router, s_bias, s_gfin = sem("s_poolw"), sem("s_router"), sem("s_bias"), sem("s_gfin")
        s_tsmall, s_small = sem("s_tsmall"), sem("s_small")
        s_ss, s_rs, s_xr, s_tx, s_xnT = (sem(n) for n in ("s_ss", "s_rs", "s_xr", "s_tx", "s_xnT"))
        s_proj, s_sig, s_glu, s_u, s_convp, s_convs, s_z, s_pm, s_pool = (
            sem(n) for n in ("s_proj", "s_sig", "s_glu", "s_u", "s_convp", "s_convs", "s_z", "s_pm", "s_pool"))
        s_tail, s_tailev, s_cache, s_lnf, s_var, s_std, s_nrm, s_lnb, s_conv = (
            sem(n) for n in ("s_tail", "s_tailev", "s_cache", "s_lnf", "s_var", "s_std", "s_nrm", "s_lnb", "s_conv"))
        s_op, s_h, s_ss2, s_rs2, s_hr, s_rt, s_hnT, s_log, s_mask = (
            sem(n) for n in ("s_op", "s_h", "s_ss2", "s_rs2", "s_hr", "s_rt", "s_hnT", "s_log", "s_mask"))
        s_vs, s_exp, s_rank, s_ab, s_inv, s_tab = (sem(n) for n in ("s_vs", "s_exp", "s_rank", "s_ab", "s_inv", "s_tab"))
        s_idx, s_sel, s_txd, s_xT, s_gu, s_gs, s_free, s_act, s_hdn = (
            sem(n) for n in ("s_idx", "s_sel", "s_txd", "s_xT", "s_gu", "s_gs", "s_free", "s_act", "s_hdn"))
        s_up, s_thd, s_hT, s_down, s_y, s_bump = (sem(n) for n in ("s_up", "s_thd", "s_hT", "s_down", "s_y", "s_bump"))
        s_xg = [sem(f"s_xg{i}") for i in range(2)]
        s_yst = [sem(f"s_yst{i}") for i in range(2)]
        s_gat = [sem(f"s_gat{i}") for i in range(J)]
        s_comb, s_ss3, s_rs3, s_fin, s_out = (sem(n) for n in ("s_comb", "s_ss3", "s_rs3", "s_fin", "s_out"))
        s_L = sem("s_L")
        s_hrst = [sem(f"s_hrst{i}") for i in range(2)]
        s_tout = [sem(f"s_tout{i}") for i in range(2)]
        s_newest = sem("s_newest")
        s_row = sem("s_row")
        s_issued = sem("s_issued")
        s_chain = sem("s_chain")

        block = ctx.enter_context(nc.Block(no_gpsimd_drain=True))

        RING_BASE = [48, 48, 32, 32, 32, 32, 16, 16]

        def slot_of(c0):
            return (c0 + MIX_CHUNKS) % RING

        def landed(c0, it):
            s = slot_of(c0)
            uses = (c0 + MIX_CHUNKS) // RING - (2 if s < 2 else 1) + 1
            return RING_BASE[s] + 16 * uses + it * (16 * 2 * (GU_CHUNKS + DN_CHUNKS) // RING)

        def gu_chunk(i0):
            return 0 if i0 == 0 else 12 * i0 - 4

        def dn_chunk(i0):
            return 12 * i0 + 16

        def choices(j):
            s = 2 * j % RING
            return ring[0:rows[j], s:s + 2, :].rearrange("p s n -> p (s n)")

        def n_loops(eng):
            eng.wait_ge(s_tab, 2)
            return eng.value_load(nit_i[0:1, 1:2], min_val=E // 2 - 1, max_val=(E + MAX_OVER) // 2 - 1)

        def chunk_view(s, a):
            return ring[:, s, :].rearrange("p (a n) -> p a n", a=a)

        @block.sync
        def _(sp):
            for j in range(J):
                src = x_prompt[0, j * P:(j + 1) * P, :] if j < J - 1 else x_sample.rearrange("b t d -> (b t) d")
                sp.dma_start(h[0:rows[j], j, :], src).then_inc(s_x[j], 16)
            win = w_in[0].rearrange("(k p) n -> p k n", p=P)
            for q in range(IN_CHUNKS):
                for a in range(2):
                    col = CH + (a * G + q) * P if q < G else ((q - G) * 2 + a) * P
                    dst = ring[:, q, a * K * P:(a + 1) * K * P].rearrange("p (k n) -> p k n", k=K)
                    sp.dma_start(dst, win[:, :, col:col + P]).then_inc(s_ring[q], 16)
            for m in range(OUT_CHUNKS):
                n = IN_CHUNKS + m
                if n >= RING:
                    sp.wait_ge(s_used, n - RING + 1)
                sp.dma_start(chunk_view(n % RING, 2),
                             w_out[0].rearrange("(k p) n -> p k n", p=P)[:, 2 * m:2 * m + 2, :]).then_inc(s_ring[n % RING], 16)

            def load(c0, it, src, a):
                sp.wait_ge(s_used, c0 + MIX_CHUNKS - RING + 1 + 24 * it)
                dst = chunk_view(slot_of(c0), a) if a > 1 else ring[:, slot_of(c0), :]
                sp.dma_start(dst, src).then_inc(s_ring[slot_of(c0)], 16)

            def load_gu(i0, it, e):
                w = w_gate_up[0, bass.ds(e, 1), :, :].rearrange("a (k p) n -> p (a k) n", p=P)
                for k in range(GU_CHUNKS):
                    load(gu_chunk(i0) + k, it, w[:, k, :], 1)

            def load_dn(i0, it, e, c0=None):
                w = w_down[0, bass.ds(e, 1), :, :].rearrange("a (k p) n -> p (a k) n", p=P)
                for m in range(DN_CHUNKS):
                    load((dn_chunk(i0) if c0 is None else c0) + m, it, w[:, 2 * m:2 * m + 2, :], 2)

            load_gu(0, 0, 0)
            load_gu(1, 0, 1)
            load_dn(0, 0, 0)
            nit = n_loops(sp)
            with sp.Fori(0, nit) as it:
                e = [sp.value_load(blk_i[0:1, bass.ds(2 * it + n, 1)], min_val=0, max_val=E - 1) for n in (1, 2, 3)]
                for u in range(2):
                    load_gu(2 + u, it, e[u + 1])
                    load_dn(1 + u, it, e[u])
            e = sp.value_load(blk_i[0:1, bass.ds(2 * nit + 1, 1)], min_val=0, max_val=E - 1)
            load_dn(1, nit, e, c0=gu_chunk(2))
            sp.wait_ge(s_down, 2 + 2 * nit)
            sp.wait_ge(s_yst[0], 16 * (nit + 1))
            sp.wait_ge(s_yst[1], 16 * (nit + 1))
            for j in range(J):
                if j >= RING // 2:
                    sp.wait_ge(s_comb, TOP_K * (j - RING // 2 + 1))
                sp.dma_start(choices(j), rows_dram[j * P * TOP_K:(j * P + rows[j]) * TOP_K, :].rearrange("(p k) n -> p (k n)", k=TOP_K)
                             ).then_inc(s_gat[j], 16)

        @block.gpsimd
        def _(g):
            g.memset(ident[:], 0.0).then_inc(s_pad, 1)
            g.memset(before[:], 1.0).then_inc(s_pad, 1)
            g.memset(u_p[:, :, 0:PB], 0.0).then_inc(s_pad, 1)
            g.memset(glu_p[:, :, 0:CB], 0.0).then_inc(s_pad, 1)
            g.memset(ss[:], 1.0).then_inc(s_pad, 1)
            g.memset(mv[:], 1.0).then_inc(s_pad, 1)
            g.memset(L[:], 0.0).then_inc(s_pad, 1)
            g.memset(eps[:], RMS_EPS).then_inc(s_pad, 1)
            g.memset(ones[:], 1.0).then_inc(s_cst, 1)
            g.iota(iota_s[:], pattern=[[1, P]], base=0, channel_multiplier=0, allow_small_or_imprecise_dtypes=True).then_inc(s_cst, 1)
            g.iota(tokid[:], pattern=[[P, J]], base=0, channel_multiplier=1, allow_small_or_imprecise_dtypes=True).then_inc(s_cst, 1)
            g.iota(base1[:], pattern=[[P, E]], base=0, channel_multiplier=0, allow_small_or_imprecise_dtypes=True).then_inc(s_cst, 1)
            g.iota(part[:], pattern=[[0, 1]], base=0, channel_multiplier=1, allow_small_or_imprecise_dtypes=True).then_inc(s_cst, 1)
            g.iota(nth[:], pattern=[[1, TOP_K]], base=1, channel_multiplier=0, allow_small_or_imprecise_dtypes=True).then_inc(s_cst, 1)
            g.iota(inv[:], pattern=[[1, PB]], base=1, channel_multiplier=0, allow_small_or_imprecise_dtypes=True).then_inc(s_cst, 1)
            g.wait_ge(s_pad, 8)
            g.affine_select(out=ident[:], in_=ident[:], compare_op=ALU.not_equal, fill=1.0, base=0,
                            pattern=[[-1, P]], channel_multiplier=1).then_inc(s_cst, 1)
            g.affine_select(out=before[:], in_=before[:], compare_op=ALU.is_gt, fill=0.0, base=0,
                            pattern=[[1, P]], channel_multiplier=-1).then_inc(s_cst, 1)

            def gather(n0, it):
                n = n0 + 2 * it
                b = n0 % 2
                g.wait_ge(s_idx, n + 1)
                if n0 >= 2:
                    g.wait_ge(s_txd, n - 1)
                g.sem_inc(s_issued, 1)
                g.indirect_dma_start(row_buf[b][:, :], None, normed_dram[:, :],
                                     bass.IndirectOffsetOnAxis(ap=idx_cur[b][:, 0:1], axis=0),
                                     bounds_check=T - 1, oob_is_err=False).then_inc(s_xg[b], 16)

            def scatter(i0, it):
                i, b = i0 + 2 * it, i0 % 2
                g.wait_ge(s_row, i + 1)
                g.wait_ge(s_y, i + 1)
                g.sem_inc(s_issued, 1)
                g.indirect_dma_start(rows_dram[:, :], bass.IndirectOffsetOnAxis(ap=row_cur[b][:, 0:1], axis=0),
                                     y_sb[b][:, :], None, bounds_check=TOP_K * T - 1, oob_is_err=False).then_inc(s_yst[b], 16)

            for n, (src, own, ready) in enumerate(((u_s, PB, s_u), (glu_s, CB, s_glu))):
                g.wait_ge(ready, 2 * G)
                g.tensor_copy(newest[n].rearrange("p c (b t) -> p c b t", b=NB), src[:, :, :, own:]).then_inc(s_newest, 1)
            g.wait_ge(s_hrst[0], 16 * 3)
            g.wait_ge(s_hrst[1], 16 * 2)
            for n0 in range(3):
                gather(n0, 0)
            scatter(0, 0)
            nit = n_loops(g)
            with g.Fori(0, nit) as it:
                for u in range(2):
                    gather(3 + u, it)
                    scatter(1 + u, it)
            scatter(1, nit)

        @block.scalar
        def _(act):
            for n, (v, a) in enumerate(((g_mix, 8), (g_moe, 8), (pool_scale, 4), (conv_b, 4), (conv_ln_g, 4), (conv_ln_b, 4))):
                r = (0, 8, 16, 20, 24, 28)[n]
                act.dma_start(vec_rows[r:r + a, :], v[0].rearrange("(k p) -> k p", p=P)).then_inc(s_vec, 16)
            act.dma_start(cw_rows, conv_w[0]).then_inc(s_vec, 16)
            act.dma_start(sp_rows, state_pool[0].rearrange("b r c -> (b r) c")).then_inc(s_vec, 16)
            for a in range(2):
                act.dma_start(sc_rows[:, a, :], state_conv[0, a * NB // 2:(a + 1) * NB // 2].rearrange("b r c -> (b r) c")).then_inc(s_vec, 16)
            act.dma_start(poolw[:], pool_w[0].rearrange("g p n -> p g n")).then_inc(s_poolw, 16)
            act.dma_start(router[:], w_router[0].rearrange("(k p) n -> p k n", p=P)).then_inc(s_router, 16)
            act.dma_start(br[:], b_router.to_broadcast([P, E])).then_inc(s_router, 16)
            act.dma_start(bias[:, 0:2 * FF], b_gate_up[0]).then_inc(s_bias, 16)
            act.dma_start(bias[:, 2 * FF:], b_down[0]).then_inc(s_bias, 16)
            act.dma_start(pool_sample[0, :, 0:PB - NT, :], state_pool[0, :, NT:, :]).then_inc(s_cache, 16)
            act.dma_start(conv_sample[0, :, 0:CB - NT, :], state_conv[0, :, NT:, :]).then_inc(s_cache, 16)

            def squares(src, out, r, s):
                return act.activation(out=s, in_=src, func=ACT.Square, accum_out=out)

            act.wait_ge(s_pad, 8)
            for j in range(J):
                act.wait_ge(s_x[j], 16)
                act.activation(out=flat[0:rows[j], 0:D], in_=h[0:rows[j], j, :], func=ACT.Square,
                               accum_out=ss[0:rows[j], 0, j:j + 1]).then_inc(s_ss, 1)
                act.wait_ge(s_ss, j + 1)
            act.activation(out=ss[:, 1, :], in_=ss[:, 0, :], func=ACT.Sqrt, scale=1.0 / D, bias=eps[:]).then_inc(s_ss, 1)
            act.wait_ge(s_rs, 1)
            for j in range(J):
                if j >= 2:
                    act.wait_ge(s_tx, 2 * (j - 1))
                act.activation(out=row_buf[j % 2][0:rows[j], :], in_=h[0:rows[j], j, :], func=ACT.Copy,
                               scale=ss[0:rows[j], 2, j:j + 1]).then_inc(s_xr, 1)
            for q in range(G):
                act.wait_ge(s_proj, q + 1)
                if q >= 2:
                    act.wait_ge(s_glu, 2 * (q - 1))
                b = 2 + 2 * (q % 2)
                act.activation(out=sig_p[q % 2][:, 0:SEQ], in_=ps[:, b + 1, :], func=ACT.Sigmoid).then_inc(s_sig, 1)
                act.activation(out=sig_p[q % 2][:, SEQ:T], in_=ps[:, 6 + q % 2, NS:2 * NS], func=ACT.Sigmoid).then_inc(s_sig, 1)
            act.wait_ge(s_small, 5)
            for q in range(G, IN_CHUNKS):
                act.wait_ge(s_proj, q + 1)
                for a in range(2):
                    g_ = 2 * (q - G) + a
                    b = 2 + 2 * (q % 2)
                    act.activation(out=u_p[:, g_, PB:], in_=ps[:, b + a, :], func=ACT.Copy).then_inc(s_u, 1)
                    act.activation(out=u_s[:, g_, :, PB:],
                                   in_=ps[:, 6 + q % 2, a * NS:(a + 1) * NS].rearrange("p (b t) -> p b t", b=NB),
                                   func=ACT.Copy).then_inc(s_u, 1)

            def tail(n, bank, r, dma):
                act.wait_ge(s_tail, n + 1)
                if n >= 2:
                    act.wait_ge(s_tout[n % 2], 16)
                act.activation(out=tails[n % 2][0:r, :], in_=ps[0:r, bank, :], func=ACT.Copy).then_inc(s_tailev, 1)
                act.wait_ge(s_tailev, n + 1)
                act.dma_start(dma, tails[n % 2][0:r, :]).then_inc(s_tout[n % 2], 16)
            act.wait_ge(s_tsmall, 1)
            tail(0, 0, PB, pool_prompt[0, 0])
            tail(1, 1, NS, pool_sample[0, :, PB - NT:, :])
            for g_ in range(G):
                act.wait_ge(s_pm, g_ + 1)
                act.activation(out=yT[:, g_, 0:SEQ], in_=ps[:, 2 + g_, :], func=ACT.Copy, scale=pscale[:, g_:g_ + 1]).then_inc(s_pool, 1)
                act.activation(out=yT[:, g_, SEQ:T], in_=ps[:, 6 + g_ % 2, 0:NS], func=ACT.Copy,
                               scale=pscale[:, g_:g_ + 1]).then_inc(s_pool, 1)
            tail(2, 7, CB, conv_prompt[0, 0])
            tail(3, 0, NS, conv_sample[0, :, CB - NT:, :])
            act.wait_ge(s_var, J)
            act.activation(out=lnr[:, 0, :], in_=mv[:, :, 1], func=ACT.Sqrt, bias=eps[:]).then_inc(s_std, 1)
            for j in range(J):
                act.wait_ge(s_lnb, j + 1)
                for c in range(G):
                    act.activation(out=yT[:, G + c, j * P:j * P + rows[j]], in_=ps[:, 4 + j % 2, c * P:c * P + rows[j]],
                                   func=ACT.Silu, scale=lng[:, c:c + 1], bias=lnb[:, c:c + 1]).then_inc(s_conv, 1)
            for j in range(J):
                r = rows[j]
                act.wait_ge(s_h, j + 1)
                act.activation(out=flat[0:r, 0:D], in_=h[0:r, j, :], func=ACT.Square,
                               accum_out=ss[0:r, 0, j:j + 1]).then_inc(s_ss2, 1)
                act.wait_ge(s_ss2, 2 * j + 1)
                act.activation(out=ss[0:r, 1, j:j + 1], in_=ss[0:r, 0, j:j + 1], func=ACT.Sqrt, scale=1.0 / D,
                               bias=eps[0:r, :]).then_inc(s_ss2, 1)
                act.wait_ge(s_rs2, j + 1)
                if j >= 2:
                    act.wait_ge(s_rt, 2 * (j - 1))
                    act.wait_ge(s_hrst[j % 2], 16 * (j // 2))
                act.activation(out=row_buf[j % 2][0:r, :], in_=h[0:r, j, :], func=ACT.Copy,
                               scale=ss[0:r, 3, j:j + 1]).then_inc(s_hr, 1)
                act.wait_ge(s_hr, j + 1)
                act.dma_start(normed_dram[j * P:j * P + r, :], row_buf[j % 2][0:r, :]).then_inc(s_hrst[j % 2], 16)
            act.dma_start(gfin, g_final.rearrange("(a n) -> a n", a=1).to_broadcast([P, D])).then_inc(s_gfin, 16)
            act.wait_ge(s_vs, 1)
            act.activation(out=gates[:], in_=dmod[:, 0], func=ACT.Exp).then_inc(s_exp, 1)

            def sigmoid(i0, it):
                act.wait_ge(s_gs, i0 + 1 + 2 * it)
                act.activation(out=sig_s, in_=gate_s, func=ACT.Sigmoid, scale=ALPHA).then_inc(s_act, 1)

            def hidden(i0, it):
                act.wait_ge(s_thd, i0 + 1 + 2 * it)
                act.activation(out=spare[:, 0:FF], in_=ps[:, 0:2, :].rearrange("p b n -> p (b n)"),
                               func=ACT.Copy).then_inc(s_hT, 1)

            def result(i0, it):
                act.wait_ge(s_row, i0 + 1 + 2 * it)
                act.wait_ge(s_down, i0 + 1 + 2 * it)
                act.activation(out=y_sb[i0 % 2][:], in_=psd, func=ACT.Copy).then_inc(s_y, 1)

            act.wait_ge(s_cache, 32)
            for n in range(2):
                act.wait_ge(s_tout[n], 32)
            act.wait_ge(s_bump, 1)
            sigmoid(0, 0)
            hidden(0, 0)
            sigmoid(1, 0)
            result(0, 0)
            hidden(1, 0)
            nit = n_loops(act)
            with act.Fori(0, nit) as it:
                sigmoid(2, it)
                result(1, it)
                hidden(2, it)
                sigmoid(3, it)
                result(2, it)
                hidden(3, it)
            result(1, nit)

            for j in range(J):
                r = rows[j]
                act.wait_ge(s_comb, TOP_K * (j + 1))
                act.activation(out=flat[0:r, 0:D], in_=h[0:r, j, :], func=ACT.Square,
                               accum_out=ss[0:r, 0, j:j + 1]).then_inc(s_ss3, 1)
                act.wait_ge(s_ss3, 2 * j + 1)
                act.activation(out=ss[0:r, 1, j:j + 1], in_=ss[0:r, 0, j:j + 1], func=ACT.Sqrt, scale=1.0 / D,
                               bias=eps[0:r, :]).then_inc(s_ss3, 1)
                act.wait_ge(s_fin, j + 1)
                dst = y_prompt[0, j * P:(j + 1) * P, :] if j < J - 1 else y_sample.rearrange("b t d -> (b t) d")
                act.dma_start(dst, h[0:r, j, :]).then_inc(s_out, 16)
            act.wait_ge(s_out, 16 * J)

        @block.vector
        def _(dve):
            chain = [0]

            def link(ins):
                chain[0] += 1
                ins.then_inc(s_chain, 1)
                dve.wait_ge(s_chain, chain[0])

            dve.wait_ge(s_cst, 9)
            link(dve.reciprocal(inv[:], inv[:]))
            dve.wait_ge(s_tsmall, 1)
            dve.tensor_copy(vecT[:], ps[:, 0, 0:32]).then_inc(s_small, 1)
            dve.tensor_copy(cwT[:].rearrange("p c t -> p (c t)"), ps[:, 0, 32:32 + G * TAPS]).then_inc(s_small, 1)
            dve.tensor_copy(u_s[:, :, :, 0:PB], ps[:, 1, 0:G * NB * PB].rearrange("p (c b r) -> p c b r", c=G, b=NB)).then_inc(s_small, 1)
            for a in range(2):
                dve.tensor_copy(glu_s[:, :, a * NB // 2:(a + 1) * NB // 2, 0:CB],
                                ps[:, 2 + a, 0:G * NB // 2 * CB].rearrange("p (c b r) -> p c b r", c=G, b=NB // 2)).then_inc(s_small, 1)
            dve.wait_ge(s_ss, J + 1)
            dve.wait_ge(s_small, 5)
            dve.reciprocal(ss[:, 2, :], ss[:, 1, :]).then_inc(s_rs, 1)

            def scaled(out, half, gT, r):
                return dve.tensor_tensor(out, ps[:, half, :].rearrange("p (k t) -> p k t", k=HALF)[:, :, 0:r],
                                         gT[:, HALF * half:HALF * half + HALF].unsqueeze(2).to_broadcast([P, HALF, r]), ALU.mult)

            for j in range(J):
                for half in range(2):
                    dve.wait_ge(s_tx, 2 * j + half + 1)
                    scaled(xnT[:, HALF * half:HALF * half + HALF, j * P:j * P + rows[j]], half, gmixT, rows[j]).then_inc(s_xnT, 1)

            dve.wait_ge(s_pad, 8)
            with dve.Fori(0, G // 2) as it:
                for n in range(2):
                    q = 2 * it + n
                    b = 2 + 2 * n
                    dve.wait_ge(s_sig, 4 * it + 2 * n + 2)
                    dve.tensor_tensor(glu_p[:, bass.ds(q, 1), CB:].rearrange("p a t -> p (a t)"), ps[:, b, :],
                                      sig_p[n][:, 0:SEQ], ALU.mult).then_inc(s_glu, 1)
                    dve.tensor_tensor(glu_s[:, bass.ds(q, 1), :, CB:].rearrange("p a b t -> p (a b) t"),
                                      ps[:, 6 + n, 0:NS].rearrange("p (b t) -> p b t", b=NB),
                                      sig_p[n][:, SEQ:T].rearrange("p (b t) -> p b t", b=NB), ALU.mult).then_inc(s_glu, 1)
                    dve.wait_ge(s_glu, 4 * it + 2 * n + 2)
                    acc_p = conv[:, bass.ds(q, 1), 0:SEQ].rearrange("p a t -> p (a t)")
                    acc_s = conv[:, bass.ds(q, 1), SEQ:T].rearrange("p a (b t) -> p (a b) t", b=NB)
                    for t in range(TAPS):
                        w = cwT[:, bass.ds(q, 1), t:t + 1].rearrange("p a t -> p (a t)")
                        src_p = glu_p[:, bass.ds(q, 1), t:t + SEQ].rearrange("p a t -> p (a t)")
                        src_s = glu_s[:, bass.ds(q, 1), :, t:t + NT].rearrange("p a b t -> p (a b) t")
                        if t == 0:
                            cb = convb[:, bass.ds(q, 1)]
                            dve.tensor_scalar(acc_p, src_p, w, cb, ALU.mult, ALU.add).then_inc(s_convp, 1)
                            dve.tensor_scalar(acc_s, src_s, w, cb, ALU.mult, ALU.add).then_inc(s_convs, 1)
                        else:
                            dve.wait_ge(s_convp, TAPS * 2 * it + TAPS * n + t)
                            dve.scalar_tensor_tensor(out=acc_p, in0=src_p, scalar=w, in1=acc_p, op0=ALU.mult, op1=ALU.add).then_inc(s_convp, 1)
                            dve.wait_ge(s_convs, TAPS * 2 * it + TAPS * n + t)
                            dve.scalar_tensor_tensor(out=acc_s, in0=src_s, scalar=w, in1=acc_s, op0=ALU.mult, op1=ALU.add).then_inc(s_convs, 1)

            for g_, w in enumerate(WINDOWS):
                dve.wait_ge(s_u, 2 * g_ + 2)
                src_p, src_s = u_p[:, g_, :], u_s[:, g_, :, :]
                for m in range(g_ + 1):
                    lo, sh = 2 ** (m + 1) - 1, 2 ** m
                    dve.tensor_tensor(win_s[m % 2][:, :, lo:], src_s[:, :, lo:], src_s[:, :, lo - sh:PB + NT - sh], ALU.add)
                    link(dve.tensor_tensor(win_p[m % 2][:, lo:], src_p[:, lo:], src_p[:, lo - sh:PB + SEQ - sh], ALU.add))
                    src_p, src_s = win_p[m % 2][:, :], win_s[m % 2][:, :, :]
                dve.scalar_tensor_tensor(out=z[:, g_, SEQ:T].rearrange("p (b t) -> p b t", b=NB), in0=src_s[:, :, PB:], scalar=1.0 / w,
                                         in1=u_s[:, g_, :, PB:], op0=ALU.mult, op1=ALU.subtract)
                dve.tensor_tensor(fix[:, 0:w - 1], src_p[:, PB:PB + w - 1], inv[:, 0:w - 1], ALU.mult)
                link(dve.scalar_tensor_tensor(out=z[:, g_, 0:SEQ], in0=src_p[:, PB:], scalar=1.0 / w, in1=u_p[:, g_, PB:],
                                              op0=ALU.mult, op1=ALU.subtract))
                dve.tensor_tensor(z[:, g_, 0:w - 1], fix[:, 0:w - 1], u_p[:, g_, PB:PB + w - 1], ALU.subtract).then_inc(s_z, 1)
                dve.wait_ge(s_z, g_ + 1)

            for j in range(J):
                r, bank = rows[j], (0, 1, 2, 3, 6)[j]
                dve.wait_ge(s_lnf, j + 1)
                link(dve.bn_stats(st[0:r, :], ps[0:r, bank, :]))
                dve.bn_aggr(mv[0:r, j, :], st[0:r, :]).then_inc(s_var, 1)
                dve.wait_ge(s_var, j + 1)
            dve.wait_ge(s_std, 1)
            link(dve.reciprocal(lnr[:, 1, :], lnr[:, 0, :]))
            for j in range(J):
                r, bank = rows[j], (0, 1, 2, 3, 6)[j]
                if j >= 2:
                    dve.wait_ge(s_lnb, j - 1)
                dve.tensor_scalar(sig_p[j % 2][0:r, 0:CH], ps[0:r, bank, :], mv[0:r, j, 0:1], lnr[0:r, 1, j:j + 1],
                                  ALU.subtract, ALU.mult).then_inc(s_nrm, 1)

            def scores(j):
                r = rows[j]
                for half in range(2):
                    dve.wait_ge(s_rt, 2 * j + half + 1)
                    scaled(xT[j % 2][:, HALF * half:HALF * half + HALF, 0:r], half, gmoeT, r).then_inc(s_hnT, 1)

            def topk(j):
                r = rows[j]
                dve.wait_ge(s_log, j + 1)
                dve.tensor_tensor(L[0:r, j, :], ps[0:r, 4, j * E:(j + 1) * E], br[0:r, :], ALU.add).then_inc(s_L, 1)
                dve.wait_ge(s_L, j + 1)
                link(dve.max(v8[:, j, :], L[:, j, :]))
                link(dve.max_index(i8[:, j, :], v8[:, j, :], L[:, j, :]))

            dve.wait_ge(s_router, 32)
            for j in range(J):
                r, b = rows[j], 6 - 4 * (j % 2)
                dve.wait_ge(s_op, j + 1)
                dve.tensor_tensor(h[0:r, j, :], h[0:r, j, :], ps[0:r, b:b + 2, :].rearrange("p b n -> p (b n)"), ALU.add).then_inc(s_h, 1)
                if j >= 1:
                    scores(j - 1)
                dve.wait_ge(s_ss2, 2 * j + 2)
                dve.reciprocal(ss[0:r, 3, j:j + 1], ss[0:r, 1, j:j + 1]).then_inc(s_rs2, 1)
                if j >= 1:
                    topk(j - 1)
            scores(J - 1)
            topk(J - 1)

            dve.tensor_tensor(dmod[:, 0], v8[:, :, 0:TOP_K], v8[:, :, 0:1].to_broadcast([P, J, TOP_K]), ALU.subtract).then_inc(s_vs, 1)
            link(dve.tensor_copy(idxf[:], i8[:, :, 0:TOP_K]))
            for j in range(J):
                last = dve.tensor_tensor(oh[:, j], iota_s[:, 0:E].unsqueeze(1).to_broadcast([P, TOP_K, E]),
                                         idxf[:, j, :].unsqueeze(2).to_broadcast([P, TOP_K, E]), ALU.is_equal)
            link(last)
            with nc.allow_low_precision(reason="sums of at most one 1"):
                for j in range(J):
                    last = dve.tensor_reduce(mask[:, j, :], oh[:, j].rearrange("p k e -> p e k"), AX.X, ALU.add)
                last.then_inc(s_mask, 1)
            dve.wait_ge(s_exp, 1)
            link(dve.tensor_reduce(gsum[:, 0, :], gates[:], AX.X, ALU.add))
            link(dve.reciprocal(gsum[:, 1, :], gsum[:, 0, :]))
            link(dve.tensor_tensor(gates[:], gates[:], gsum[:, 1, :].unsqueeze(2).to_broadcast([P, J, TOP_K]), ALU.mult))

            dve.wait_ge(s_rank, 1)
            cnt = ps[:, 5, J * E:(J + 1) * E]
            link(dve.tensor_scalar(over[:, 0, :], cnt, float(P), None, ALU.is_gt))
            for b in range(2, J):
                link(dve.scalar_tensor_tensor(out=over[:, 0, :], in0=cnt, scalar=float(b * P), in1=over[:, 0, :],
                                              op0=ALU.is_gt, op1=ALU.add))
            link(dve.tensor_copy(over[:, 1, :], over[:, 0, :]))
            src, sh = 1, 1
            while sh < E:
                dst = 3 - src
                dve.tensor_copy(over[:, dst, 0:sh], over[:, src, 0:sh])
                link(dve.tensor_tensor(over[:, dst, sh:], over[:, src, sh:], over[:, src, 0:E - sh], ALU.add))
                src, sh = dst, 2 * sh
            total = over[:, src, :]
            link(dve.tensor_tensor(over[:, 3, :], total, over[:, 0, :], ALU.subtract))
            link(dve.tensor_scalar(over[:, 3, :], over[:, 3, :], float(P), float(P * (E - 1)), ALU.mult, ALU.add))
            link(dve.tensor_tensor(over[:, 4, :], over[:, 3, :], base1[:], ALU.subtract))
            for j in range(J):
                rank = ps[:, 5, j * E:(j + 1) * E]
                link(dve.scalar_tensor_tensor(out=dest[:, j, :], in0=rank, scalar=float(P), in1=over[:, 4, :],
                                              op0=ALU.is_ge, op1=ALU.mult))
                link(dve.tensor_tensor(dest[:, j, :], dest[:, j, :], rank, ALU.add))
                link(dve.tensor_tensor(dest[:, j, :], dest[:, j, :], base1[:], ALU.add))
                link(dve.tensor_tensor(oh[:, j], oh[:, j], dest[:, j, :].unsqueeze(1).to_broadcast([P, TOP_K, E]), ALU.mult))
                link(dve.tensor_reduce(dest4[:, j, :], oh[:, j], AX.X, ALU.add))
            link(dve.tensor_copy(desti[:, 0], dest4[:]))
            dve.tensor_scalar(desti[:, 1], desti[:, 0], 7, None, ALU.arith_shift_right)
            link(dve.tensor_scalar(desti[:, 2], desti[:, 0], P - 1, None, ALU.bitwise_and))
            dve.tensor_copy(dmod[:, 1], desti[:, 1])
            link(dve.tensor_copy(dmod[:, 0], desti[:, 2]))
            for j in range(J):
                if j:
                    dve.wait_ge(s_inv, j)
                dve.tensor_tensor(inA, iota_s[:].unsqueeze(1).to_broadcast([P, TOP_K, P]),
                                  dmod[:, 0, j, :].unsqueeze(2).to_broadcast([P, TOP_K, P]), ALU.is_equal)
                link(dve.tensor_tensor(inB[:, :, 0, :], iota_s[:, 0:COLS].unsqueeze(1).to_broadcast([P, TOP_K, COLS]),
                                       dmod[:, 1, j, :].unsqueeze(2).to_broadcast([P, TOP_K, COLS]), ALU.is_equal))
                link(dve.tensor_tensor(inB[:, :, 1, :], inB[:, :, 0, :], nth[:].unsqueeze(2).to_broadcast([P, TOP_K, COLS]), ALU.mult))
                dve.tensor_scalar(inB[:, :, 0, :], inB[:, :, 0, :], tokid[:, j:j + 1], None, ALU.mult).then_inc(s_ab, 1)
            dve.tensor_copy(blk_e[:, 0:E], iota_s[:, 0:E])
            link(dve.tensor_tensor(cmp[:], iota_s[:, 0:COLS - E].unsqueeze(2).to_broadcast([P, COLS - E, E]),
                                   total.unsqueeze(1).to_broadcast([P, COLS - E, E]), ALU.is_ge))
            link(dve.tensor_reduce(blk_e[:, E:], cmp[:], AX.X, ALU.add))
            link(dve.tensor_scalar(blk_e[:, E:], blk_e[:, E:], float(E - 1), None, ALU.min))
            link(dve.tensor_scalar(selm[:], blk_e[0:E, :], part[0:E, :], None, ALU.is_equal))
            dve.tensor_copy(blk_i[:], blk_e[0:1, :]).then_inc(s_tab, 1)
            link(dve.tensor_scalar(nit_f[:, 0:1], total[:, E - 1:E], float(E - 1), None, ALU.add))
            link(dve.tensor_copy(nit_i[:, 0:1], nit_f[:, 0:1]))
            dve.tensor_scalar(nit_i[:, 1:2], nit_i[:, 0:1], 1, None, ALU.arith_shift_right).then_inc(s_tab, 1)
            dve.wait_ge(s_inv, J)
            choice = ps[:, 4, J * E + COLS:J * E + 2 * COLS]
            link(dve.tensor_scalar(none[:], choice, 0.0, float(NO_ROW), ALU.is_equal, ALU.mult))
            link(dve.tensor_tensor(tok_f[:], ps[:, 4, J * E:J * E + COLS], none[:], ALU.add))
            link(dve.tensor_copy(slot_tok[:], tok_f[:]))
            link(dve.tensor_scalar(tok_f[:], tok_f[:], float(TOP_K), -1.0, ALU.mult, ALU.add))
            link(dve.tensor_tensor(slot_row[:], tok_f[:], choice, ALU.add))

            def tokens(i0, it):
                b = i0 % 2
                if i0 >= 2:
                    dve.wait_ge(s_xg[b], 16 * (i0 // 2) + 16 * it)
                dve.tensor_copy(idx_cur[b][:], slot_tok[:, bass.ds(i0 + 2 * it, 1)]).then_inc(s_idx, 1)

            def places(i0, it):
                b = i0 % 2
                if i0 >= 2:
                    dve.wait_ge(s_yst[b], 16 * (i0 // 2) + 16 * it)
                dve.tensor_copy(row_cur[b][:], slot_row[:, bass.ds(i0 + 2 * it, 1)]).then_inc(s_row, 1)

            def select(i0, it):
                if i0 >= 2:
                    dve.wait_ge(s_down, i0 - 1 + 2 * it)
                dve.tensor_copy(sel_cur[i0 % 2][:], selm[:, bass.ds(i0 + 2 * it, 1)].to_broadcast([E, P])).then_inc(s_sel, 1)

            def spread(i0, it):
                i = i0 + 2 * it
                dve.wait_ge(s_txd, i + 1)
                for half in range(2):
                    scaled(xT[i0 % 2][:, HALF * half:HALF * half + HALF, :], half, gmoeT, P).then_inc(s_xT, 1)

            def swiglu(i0, it):
                i = i0 + 2 * it
                dve.wait_ge(s_gu, i + 1)
                dve.tensor_scalar(gate_s, psg, LIMIT, None, ALU.min).then_inc(s_gs, 1)
                dve.tensor_scalar(up_s, psu, LIMIT, -LIMIT, ALU.min, ALU.max).then_inc(s_free, 1)
                dve.wait_ge(s_free, i + 1)
                dve.wait_ge(s_gs, i + 1)
                dve.scalar_tensor_tensor(out=up_s, in0=up_s, scalar=1.0, in1=gate_s, op0=ALU.add, op1=ALU.mult).then_inc(s_up, 1)
                dve.wait_ge(s_up, i + 1)
                dve.wait_ge(s_act, i + 1)
                dve.tensor_tensor(up_s, up_s, sig_s, ALU.mult).then_inc(s_hdn, 1)
                dve.wait_ge(s_hdn, i + 1)

            tokens(0, 0)
            tokens(1, 0)
            places(0, 0)
            places(1, 0)
            select(0, 0)
            dve.wait_ge(s_hnT, 2 * J)
            dve.engine_nop().then_inc(s_bump, 1)
            spread(0, 0)
            select(1, 0)
            for i0 in range(2):
                tokens(i0 + 2, 0)
                spread(i0 + 1, 0)
                swiglu(i0, 0)
                if i0:
                    select(2, 0)
                    places(2, 0)
            nit = n_loops(dve)
            with dve.Fori(0, nit) as it:
                for u in range(2):
                    tokens(4 + u, it)
                    spread(3 + u, it)
                    swiglu(2 + u, it)
                    select(3 + u, it)
                    places(3 + u, it)

            dve.wait_ge(s_gfin, 16)
            for j in range(J):
                r = rows[j]
                for k in range(TOP_K):
                    n = j * TOP_K + k
                    if k == 0:
                        dve.wait_ge(s_gat[j], 16)
                    if k:
                        dve.wait_ge(s_comb, n)
                    dve.scalar_tensor_tensor(out=h[0:r, j, :], in0=choices(j)[:, k * D:(k + 1) * D], scalar=gates[0:r, j, k:k + 1],
                                             in1=h[0:r, j, :], op0=ALU.mult, op1=ALU.add).then_inc(s_comb, 1)
                dve.wait_ge(s_ss3, 2 * j + 2)
                link(dve.reciprocal(ss[0:r, 2, j:j + 1], ss[0:r, 1, j:j + 1]))
                dve.scalar_tensor_tensor(out=h[0:r, j, :], in0=h[0:r, j, :], scalar=ss[0:r, 2, j:j + 1], in1=gfin[0:r, :],
                                         op0=ALU.mult, op1=ALU.mult).then_inc(s_fin, 1)

        @block.tensor
        def _(pe):
            pe.wait_ge(s_cst, 9)
            pe.wait_ge(s_vec, 16 * 10)
            pe.transpose(ps[:, 0, 0:32], vec_rows[:], ident[0:32, 0:32])
            for c in range(G):
                pe.transpose(ps[:, 0, 32 + c * TAPS:32 + (c + 1) * TAPS], cw_rows[:, c * P:(c + 1) * P], ident[0:TAPS, 0:TAPS])
                n = NB * PB
                pe.transpose(ps[:, 1, c * n:(c + 1) * n], sp_rows[:, c * P:(c + 1) * P], ident[0:n, 0:n])
                n = NB // 2 * CB
                for a in range(2):
                    last = pe.transpose(ps[:, 2 + a, c * n:(c + 1) * n], sc_rows[:, a, c * P:(c + 1) * P], ident[0:n, 0:n])
            last.then_inc(s_tsmall, 1)
            pe.wait_ge(s_small, 5)

            def turn(src, r, first, ready, done):
                for half in range(2):
                    if first is not None:
                        pe.wait_ge(ready, first + half)
                    for m in range(HALF):
                        k = HALF * half + m
                        last = pe.transpose(ps[:, half, m * P:m * P + r], src[0:r, k * P:(k + 1) * P], ident[0:r, 0:r])
                    last.then_inc(done, 1)

            for j in range(J):
                pe.wait_ge(s_xr, j + 1)
                turn(row_buf[j % 2], rows[j], 2 * j - 1 if j else None, s_xnT, s_tx)
            pe.wait_ge(s_xnT, 2 * J)

            for q in range(IN_CHUNKS):
                pe.wait_ge(s_ring[q], 32)
                b = 2 + 2 * (q % 2)
                if q in (2, 3, 4, 5):
                    pe.wait_ge(s_glu, 2 * (q - 1))
                for a in range(2):
                    w = ring[:, q, a * K * P:(a + 1) * K * P].rearrange("p (k n) -> p k n", k=K)
                    for k in range(K):
                        pe.matmul(ps[:, b + a, :], lhsT=w[:, k, :], rhs=xnT[:, k, 0:SEQ], start=k == 0, stop=k == K - 1)
                    for k in range(K):
                        last = pe.matmul(ps[:, 6 + q % 2, a * NS:(a + 1) * NS], lhsT=w[:, k, :], rhs=xnT[:, k, SEQ:T],
                                         start=k == 0, stop=k == K - 1)
                last.then_inc(s_proj, 1)
                pe.nop().then_inc(s_used, 1) if False else None
                pe.wait_ge(s_proj, q + 1)
                pe.sem_inc(s_used, 1)

            pe.wait_ge(s_u, 2 * G)
            def tails_of(src, r, bank):
                for c in range(G):
                    last = pe.transpose(ps[0:r, bank, c * P:(c + 1) * P], src(c), ident[:])
                last.then_inc(s_tail, 1)
            tails_of(lambda c: u_p[:, c, PB + SEQ - PB:], PB, 0)
            pe.wait_ge(s_newest, 1)
            tails_of(lambda c: newest[0][:, c, :], NS, 1)
            pe.wait_ge(s_poolw, 16)
            for g_ in range(G):
                pe.wait_ge(s_z, g_ + 1)
                pe.matmul(ps[:, 2 + g_, :], lhsT=poolw[:, g_, :], rhs=z[:, g_, 0:SEQ], start=True, stop=True)
                if g_ >= 2:
                    pe.wait_ge(s_pool, 2 * (g_ - 1))
                pe.matmul(ps[:, 6 + g_ % 2, 0:NS], lhsT=poolw[:, g_, :], rhs=z[:, g_, SEQ:T],
                          start=True, stop=True).then_inc(s_pm, 1)
            pe.wait_ge(s_glu, 2 * G)
            pe.wait_ge(s_pool, 2 * G)
            pe.wait_ge(s_tailev, 2)
            tails_of(lambda c: glu_p[:, c, CB + SEQ - CB:], CB, 7)
            pe.wait_ge(s_newest, 2)
            tails_of(lambda c: newest[1][:, c, :], NS, 0)

            pe.wait_ge(s_convp, TAPS * G)
            pe.wait_ge(s_convs, TAPS * G)
            pe.wait_ge(s_tailev, 4)
            pe.wait_ge(s_pool, 2 * G)
            for j in range(J):
                bank = (0, 1, 2, 3, 6)[j]
                for c in range(G):
                    last = pe.transpose(ps[0:rows[j], bank, c * P:(c + 1) * P], conv[:, c, j * P:j * P + rows[j]], ident[:])
                last.then_inc(s_lnf, 1)
            for j in range(J):
                r = rows[j]
                pe.wait_ge(s_nrm, j + 1)
                if j >= 2:
                    pe.wait_ge(s_conv, G * (j - 1))
                for c in range(G):
                    last = pe.transpose(ps[:, 4 + j % 2, c * P:c * P + r], sig_p[j % 2][0:r, c * P:(c + 1) * P], ident[0:r, 0:r])
                last.then_inc(s_lnb, 1)

            def wout(k):
                return chunk_view((IN_CHUNKS + k // 2) % RING, 2)[:, k % 2, :]

            def output(j):
                r, b = rows[j], 6 - 4 * (j % 2)
                pe.wait_ge(s_conv, G * (j + 1))
                if j >= 2:
                    pe.wait_ge(s_h, j - 1)
                for k in range(K):
                    for n in range(2):
                        last = pe.matmul(ps[0:r, b + n, :], lhsT=yT[:, k, j * P:j * P + r], rhs=wout(k)[:, n * 512:(n + 1) * 512],
                                         start=k == 0, stop=k == K - 1)
                last.then_inc(s_op, 1)

            def logits(j):
                r = rows[j]
                pe.wait_ge(s_hr, j + 1)
                turn(row_buf[j % 2], r, 2 * j - 1 if j else None, s_hnT, s_rt)
                pe.wait_ge(s_hnT, 2 * j + 2)
                if j:
                    pe.wait_ge(s_L, j)
                for k in range(K):
                    last = pe.matmul(ps[0:r, 4, j * E:(j + 1) * E], lhsT=xT[j % 2][:, k, 0:r], rhs=router[:, k, :],
                                     start=k == 0, stop=k == K - 1)
                last.then_inc(s_log, 1)

            pe.wait_ge(s_ring[6], 16)
            pe.wait_ge(s_ring[7], 16)
            pe.wait_ge(s_ring[0], 48)
            pe.wait_ge(s_ring[1], 48)
            pe.wait_ge(s_router, 32)
            pe.wait_ge(s_nrm, J)
            output(0)
            output(1)
            pe.wait_ge(s_conv, G * J)
            for j in range(J):
                logits(j)
                if j + 2 < J:
                    output(j + 2)
                if j + 2 == J - 1:
                    pe.wait_ge(s_op, J)
                    for _ in range(OUT_CHUNKS):
                        pe.sem_inc(s_used, 1)

            pe.wait_ge(s_mask, 1)
            for j in range(J):
                for i in range(j):
                    pe.matmul(ps[:, 5, j * E:(j + 1) * E], lhsT=ones[:], rhs=mask[:, i, :], start=i == 0, stop=False)
                r = rows[j]
                pe.matmul(ps[:, 5, j * E:(j + 1) * E], lhsT=before[0:r, :], rhs=mask[0:r, j, :], start=j == 0, stop=True)
            for j in range(J):
                r = rows[j]
                last = pe.matmul(ps[:, 5, J * E:(J + 1) * E], lhsT=ones[0:r, :], rhs=mask[0:r, j, :], start=j == 0, stop=j == J - 1)
            last.then_inc(s_rank, 1)
            for j in range(J):
                r = rows[j]
                pe.wait_ge(s_ab, j + 1)
                for k in range(TOP_K):
                    last = pe.matmul(ps[:, 4, J * E:J * E + 2 * COLS], lhsT=inA[0:r, k, :], rhs=inB[0:r, k, :, :],
                                     start=j == 0 and k == 0, stop=j == J - 1 and k == TOP_K - 1)
                last.then_inc(s_inv, 1)

            def turn_x(i0, it):
                b, i = i0 % 2, i0 + 2 * it
                pe.wait_ge(s_xg[b], 16 * (i0 // 2 + 1) + 16 * it)
                if i0 >= 2:
                    pe.wait_ge(s_hT, i - 1)
                for k in range(K):
                    last = pe.transpose(ps[:, k // HALF, k % HALF * P:(k % HALF + 1) * P], row_buf[b][:, k * P:(k + 1) * P], ident[:])
                last.then_inc(s_txd, 1)

            def turn_h(i0, it):
                i = i0 + 2 * it
                pe.wait_ge(s_hdn, i + 1)
                pe.wait_ge(s_xT, 2 * i + 4)
                for k in range(KF):
                    last = pe.transpose(ps[:, k // HALF, k % HALF * P:(k % HALF + 1) * P], up_s[:, k * P:(k + 1) * P], ident[:])
                last.then_inc(s_thd, 1)

            def gate_up(i0, it):
                i, b = i0 + 2 * it, i0 % 2
                pe.wait_ge(s_xT, 2 * i + 2)
                pe.wait_ge(s_sel, i + 1)
                if i0:
                    pe.wait_ge(s_free, i)
                    pe.wait_ge(s_gs, i)
                for n in range(4):
                    pe.matmul(ps[:, 4 + n, :], lhsT=sel_cur[b][:], rhs=bias[:, n * 512:(n + 1) * 512], start=True, stop=False)
                for k in range(K):
                    c = gu_chunk(i0) + k
                    pe.wait_ge(s_ring[slot_of(c)], landed(c, it))
                    for n in range(4):
                        last = pe.matmul(ps[:, 4 + n, :], lhsT=xT[b][:, k, :], rhs=ring[:, slot_of(c), n * 512:(n + 1) * 512],
                                         start=False, stop=k == K - 1)
                    last.then_inc(s_used if k < K - 1 else s_gu, 1)
                pe.wait_ge(s_gu, i + 1)
                pe.sem_inc(s_used, 1)

            def down(i0, it, c0=None):
                i, b = i0 + 2 * it, i0 % 2
                pe.wait_ge(s_hT, i + 1)
                if i0:
                    pe.wait_ge(s_y, i)
                for n in range(2):
                    pe.matmul(ps[:, 2 + n, :], lhsT=sel_cur[b][:], rhs=bias[:, 2 * FF + n * 512:2 * FF + (n + 1) * 512],
                              start=True, stop=False)
                for k in range(KF):
                    c = (dn_chunk(i0) if c0 is None else c0) + k // 2
                    if k % 2 == 0:
                        pe.wait_ge(s_ring[slot_of(c)], landed(c, it))
                    for n in range(2):
                        last = pe.matmul(ps[:, 2 + n, :], lhsT=hT[:, k, :],
                                         rhs=chunk_view(slot_of(c), 2)[:, k % 2, n * 512:(n + 1) * 512],
                                         start=False, stop=k == KF - 1)
                    if k % 2:
                        last.then_inc(s_used if k < KF - 1 else s_down, 1)
                pe.wait_ge(s_down, i + 1)
                pe.sem_inc(s_used, 1)

            pe.wait_ge(s_bias, 32)
            pe.wait_ge(s_bump, 1)
            turn_x(0, 0)
            gate_up(0, 0)
            pe.wait_ge(s_xT, 2)
            turn_x(1, 0)
            turn_h(0, 0)
            gate_up(1, 0)
            turn_x(2, 0)
            down(0, 0)
            turn_h(1, 0)
            nit = n_loops(pe)
            with pe.Fori(0, nit) as it:
                for u in range(2):
                    gate_up(2 + u, it)
                    turn_x(3 + u, it)
                    down(1 + u, it)
                    turn_h(2 + u, it)
            down(1, nit, c0=gu_chunk(2))


_INS = ["x_prompt", "x_sample", "state_pool", "state_conv", "g_mix", "w_in", "pool_w", "pool_scale", "conv_w", "conv_b",
        "conv_ln_g", "conv_ln_b", "w_out", "g_moe", "w_router", "b_router", "w_gate_up", "b_gate_up", "w_down", "b_down",
        "g_final"]
_OUTS = [(1, 512, 1024), (8, 8, 1024), (1, 1, 15, 512), (1, 1, 30, 512), (1, 8, 15, 512), (1, 8, 30, 512)]


def kernel(**inputs):
    import numpy as _np
    import concourse.bacc as _bacc
    from concourse import mybir as _mybir
    from concourse.bass_utils import run_bass_kernel_spmd as _run

    nc = _bacc.Bacc("TRN2", target_bir_lowering=False, num_devices=1)
    arrays, args = {}, []
    for name in _INS:
        a = _np.ascontiguousarray(inputs[name])
        arrays[f"in_{name}_dram"] = a
        args.append(nc.dram_tensor(f"in_{name}_dram", a.shape, _mybir.dt.from_np(a.dtype), kind="ExternalInput").ap())
    for i, shape in enumerate(_OUTS):
        args.append(nc.dram_tensor(f"out_{i}_dram", shape, _mybir.dt.float32, kind="ExternalOutput").ap())
    args.append(nc.dram_tensor("normed_rows_dram", (576, 1024), _mybir.dt.float32, kind="Internal").ap())
    args.append(nc.dram_tensor("choice_rows_dram", (576 * 4, 1024), _mybir.dt.float32, kind="Internal").ap())
    hybrid_moe_step(nc, *args)
    r = _run(nc, [arrays], core_ids=[0])
    return tuple(r.results[0][f"out_{i}_dram"] for i in range(len(_OUTS)))
```

```python
from contextlib import ExitStack

import concourse.bass as bass
from concourse import mybir

P = 128
F32 = mybir.dt.float32
F32R = mybir.dt.float32r
F16 = mybir.dt.float16
I32 = mybir.dt.int32
U32 = mybir.dt.uint32
ALU = mybir.AluOpType
ACT = mybir.ActivationFunctionType
AX = mybir.AxisListType

WINDOWS = (2, 4, 8, 16)
TOP_K = 4
RMS_EPS = 1e-5
LN_EPS = 1e-5
NO_ROW = 1 << 16
LIMIT = 7.0
ALPHA = 1.702
RING = 4
SLOT = 2048


def hybrid_moe_step(nc, x_prompt, x_sample, state_pool, state_conv, g_mix, w_in, pool_w, pool_scale,
                    conv_w, conv_b, conv_ln_g, conv_ln_b, w_out, g_moe, w_router, b_router,
                    w_gate_up, b_gate_up, w_down, b_down, g_final,
                    y_prompt, y_sample, pool_prompt, conv_prompt, pool_sample, conv_sample,
                    normed_dram, rows_dram):
    _, SEQ, D = x_prompt.shape
    NB, NT, _ = x_sample.shape
    NS = NB * NT
    T = SEQ + NS
    CH = pool_scale.shape[1]
    G = CH // P
    TAPS = conv_w.shape[1]
    PB, CB = state_pool.shape[2], state_conv.shape[2]
    E = w_router.shape[2]
    K = D // P
    FF = w_down.shape[2]
    KF = FF // P
    rows = [P] * (SEQ // P) + [NS]
    J = len(rows)
    MAX_OVER = TOP_K * T // P
    COLS = E + MAX_OVER + 2
    GU_CHUNKS, DN_CHUNKS = K, KF // 2
    IN_CHUNKS = 6
    assert D == 1024 and CH == 512 and FF == D and SEQ == 512 and NS == 64
    assert GU_CHUNKS % RING == 0 and DN_CHUNKS == RING
    HALF = 4

    with ExitStack() as ctx:
        def sb(name, shape, dt=F32):
            return ctx.enter_context(nc.sbuf_tensor(name, shape, dt))

        def sem(name):
            return ctx.enter_context(nc.semaphore(name))

        ring = sb("ring", [P, RING, SLOT])
        h = sb("h", [P, J, D])
        row_buf = [sb(f"row_buf{i}", [P, D]) for i in range(2)]
        router = sb("router", [P, K, E])
        br = sb("br", [P, E])
        vecT = sb("vecT", [P, 32])
        cwT = sb("cwT", [P, G, TAPS])
        ident = sb("ident", [P, P])
        before = sb("before", [P, P], F16)
        ones = sb("ones", [P, P], F16)
        iota_s = sb("iota_s", [P, P])
        tokid = sb("tokid", [P, J])
        base1 = sb("base1", [P, E])
        part = sb("part", [2 * E, 1])
        low = sb("low", [2 * E, 1])
        inv = sb("inv", [P, PB])
        eps = sb("eps", [P, 1])
        ss = sb("ss", [P, 4, J])
        mv = sb("mv", [P, J, 2])
        st = sb("st", [P, 6])
        lnr = sb("lnr", [P, 2, J])
        fix = sb("fix", [P, PB])
        L = sb("L", [P, J, E])
        v8 = sb("v8", [P, J, 8])
        i8 = sb("i8", [P, J, 8], U32)
        idxf = sb("idxf", [P, J, TOP_K])
        mask = sb("mask", [P, J, E], F16)
        gates = sb("gates", [P, J, TOP_K])
        gsum = sb("gsum", [P, 2, J])
        over = sb("over", [P, 5, E])
        dest = sb("dest", [P, J, E])
        dest4 = sb("dest4", [P, J, TOP_K])
        desti = sb("desti", [P, 3, J, TOP_K], I32)
        dmod = sb("dmod", [P, 2, J, TOP_K])
        nth = sb("nth", [P, TOP_K])
        none = sb("none", [P, COLS])
        tok_f = sb("tok_f", [P, COLS])
        blk_e = sb("blk_e", [P, COLS])
        blk_i = sb("blk_i", [1, COLS], I32)
        selm = sb("selm", [2 * E, COLS])
        slot_tok = sb("slot_tok", [P, COLS], U32)
        slot_row = sb("slot_row", [P, COLS], U32)
        idx_cur = [sb(f"idx_cur{i}", [P, 1], U32) for i in range(2)]
        row_cur = [sb(f"row_cur{i}", [P, 1], U32) for i in range(2)]
        sel_cur = [sb(f"sel_cur{i}", [2 * E, P], F32R) for i in range(2)]
        nit_f = sb("nit_f", [P, 2])
        nit_i = sb("nit_i", [P, 2], I32)
        ps = ctx.enter_context(nc.psum_tensor("ps", [P, 8, 512], F32))
        psg = ps[:, 4:6, :].rearrange("p b n -> p (b n)")
        psu = ps[:, 6:8, :].rearrange("p b n -> p (b n)")
        psd = ps[:, 2:4, :].rearrange("p b n -> p (b n)")
        pst = ps[:, 0:2, :].rearrange("p b n -> p (b n)")

        with ExitStack() as mix:
            def mb(name, shape, dt=F32):
                return mix.enter_context(nc.sbuf_tensor(name, shape, dt))

            wout = mb("wout", [P, K, D])
            shared = mb("shared", [P, 2, G * T])
            u_p = mb("u_p", [P, G, PB + SEQ])
            u_s = mb("u_s", [P, G, NB, PB + NT])
            glu_p = mb("glu_p", [P, G, CB + SEQ])
            glu_s = mb("glu_s", [P, G, NB, CB + NT])
            win_p = [mb(f"win_p{i}", [P, PB + SEQ]) for i in range(2)]
            win_s = [mb(f"win_s{i}", [P, NB, PB + NT]) for i in range(2)]
            sig_p = [mb(f"sig_p{i}", [P, T]) for i in range(2)]
            stage = [mb(f"stage{i}", [P, D]) for i in range(2)]
            xT = [mb(f"xT{i}", [P, K, P]) for i in range(2)]
            vec_rows = mb("vec_rows", [32, P])
            poolw = mb("poolw", [P, G, P])
            gmoe = mb("gmoe", [P, D])
            mixT = mb("mixT", [P, K, T])
        xnT = mixT
        yT = mixT
        conv = shared[:, 0, :].rearrange("p (c t) -> p c t", c=G)
        z = shared[:, 1, :].rearrange("p (c t) -> p c t", c=G)
        junk = shared[:, 0, 0:D]
        cw_rows = stage[0][0:TAPS, CH:2 * CH]
        sp_rows = stage[0][0:NB * PB, 0:CH]
        sc_rows = stage[1][0:NB // 2 * CB, :].rearrange("p (a n) -> p a n", a=2)
        tails = [stage[0][:, 512:1024], stage[1][:, 0:512]]
        newest = [xT[i][:, 0:2, :].rearrange("p k t -> p (k t)").rearrange("p (c t) -> p c t", c=G) for i in range(2)]
        u_flat, z_flat = u_p[:].rearrange("p c t -> p (c t)"), shared[:, 1, :]
        pool_out = [u_flat[:, 0:D], u_flat[:, D:2 * D], z_flat[:, 0:D], z_flat[:, D:2 * D],
                    xT[0][:].rearrange("p k t -> p (k t)")]
        diag = row_buf[0][:, 0:J * P].rearrange("p (j t) -> p j t", j=J)
        spare = mixT[:, :, :].rearrange("p k t -> p (k t)")
        oh = spare[:, 2048:2048 + J * TOP_K * E].rearrange("p (j k e) -> p j k e", j=J, k=TOP_K)
        cmp = spare[:, 3072:3072 + (COLS - E) * E].rearrange("p (n e) -> p n e", e=E)
        inA = spare[:, 3840:3840 + TOP_K * P // 2].bitcast(F16).rearrange("p (k s) -> p k s", k=TOP_K)
        inB = spare[:, 4096:4096 + TOP_K * COLS].bitcast(F16).rearrange("p (k a n) -> p k a n", k=TOP_K, a=2)

        w_hi = sb("w_hi", [P, RING, SLOT], F32R)
        w_lo = sb("w_lo", [P, RING, SLOT], F32R)
        swi = sb("swi", [P, 3 * FF])
        bias = sb("bias", [2 * E, 2 * FF + D], F32R)
        x_hi, x_lo = sb("x_hi", [P, K, P], F32R), sb("x_lo", [P, K, P], F32R)
        h_hi, h_lo = sb("h_hi", [P, KF, P], F32R), sb("h_lo", [P, KF, P], F32R)
        y_sb = [sb(f"y_sb{i}", [P, D]) for i in range(2)]
        gfin = sb("gfin", [P, D])
        gate_s, up_s, sig_s = (swi[:, n * FF:(n + 1) * FF] for n in range(3))
        bias_raw = swi[0:2 * E, :]

        gmixT = vecT[:, 0:8]
        pscale, convb, lng, lnb = (vecT[:, 16 + 4 * n:20 + 4 * n] for n in range(4))

        s_cst = sem("s_cst")
        s_pad = sem("s_pad")
        s_vec = sem("s_vec")
        s_state = sem("s_state")
        s_x = [sem(f"s_x{j}") for j in range(J)]
        s_ring = [sem(f"s_ring{n}") for n in range(RING)]
        s_win = sem("s_win")
        s_hi, s_lo = sem("s_hi"), sem("s_lo")
        s_used = sem("s_used")
        s_wout, s_gmoe, s_biasp, s_dsel = sem("s_wout"), sem("s_gmoe"), sem("s_biasp"), sem("s_dsel")
        s_x_hi, s_x_lo, s_h_hi, s_h_lo = (sem(n) for n in ("s_x_hi", "s_x_lo", "s_h_hi", "s_h_lo"))
        s_poolw, s_router, s_bias, s_gfin = sem("s_poolw"), sem("s_router"), sem("s_bias"), sem("s_gfin")
        s_tsmall, s_small = sem("s_tsmall"), sem("s_small")
        s_ss, s_rs, s_xr, s_tx, s_xnT = (sem(n) for n in ("s_ss", "s_rs", "s_xr", "s_tx", "s_xnT"))
        s_proj, s_sig, s_glu, s_u, s_convp, s_convs, s_z, s_pm, s_pool = (
            sem(n) for n in ("s_proj", "s_sig", "s_glu", "s_u", "s_convp", "s_convs", "s_z", "s_pm", "s_pool"))
        s_tail, s_tailev, s_cache, s_lnf, s_var, s_std, s_nrm, s_lnb, s_conv = (
            sem(n) for n in ("s_tail", "s_tailev", "s_cache", "s_lnf", "s_var", "s_std", "s_nrm", "s_lnb", "s_conv"))
        s_op, s_h, s_ss2, s_rs2, s_hr, s_rt, s_hnT, s_log, s_mask = (
            sem(n) for n in ("s_op", "s_h", "s_ss2", "s_rs2", "s_hr", "s_rt", "s_hnT", "s_log", "s_mask"))
        s_vs, s_exp, s_rank, s_ab, s_inv, s_tab = (sem(n) for n in ("s_vs", "s_exp", "s_rank", "s_ab", "s_inv", "s_tab"))
        s_idx, s_sel, s_txd, s_gu, s_gs, s_free, s_act, s_hdn = (
            sem(n) for n in ("s_idx", "s_sel", "s_txd", "s_gu", "s_gs", "s_free", "s_act", "s_hdn"))
        s_thd, s_down, s_y = (sem(n) for n in ("s_thd", "s_down", "s_y"))
        s_xg = [sem(f"s_xg{i}") for i in range(2)]
        s_yst = [sem(f"s_yst{i}") for i in range(2)]
        s_gat = [sem(f"s_gat{i}") for i in range(J)]
        s_comb, s_ss3, s_rs3, s_fin, s_out = (sem(n) for n in ("s_comb", "s_ss3", "s_rs3", "s_fin", "s_out"))
        s_L = sem("s_L")
        s_hrst = [sem(f"s_hrst{i}") for i in range(2)]
        s_tout = [sem(f"s_tout{i}") for i in range(2)]
        s_newest = sem("s_newest")
        s_half, s_halfev = sem("s_half"), sem("s_halfev")
        s_row = sem("s_row")
        s_issued = sem("s_issued")
        s_chain = sem("s_chain")

        block = ctx.enter_context(nc.Block(no_gpsimd_drain=True))

        RING_BASE = [64, 64, 32, 32]
        PER_LOOP = 2 * (GU_CHUNKS + DN_CHUNKS)

        def gu_chunk(i0):
            return 0 if i0 == 0 else 12 * i0 - 4

        def dn_chunk(i0, last=False):
            return 12 * i0 + (8 if last else 16)

        def landed(c0, it):
            return RING_BASE[c0 % RING] + 16 * (c0 // RING + 1) + 16 * PER_LOOP // RING * it

        def choices(j):
            s = 2 * j % RING
            return ring[0:rows[j], s:s + 2, :].rearrange("p s n -> p (s n)")

        def n_loops(eng):
            eng.wait_ge(s_tab, 2)
            return eng.value_load(nit_i[0:1, 1:2], min_val=E // 2 - 1, max_val=(E + MAX_OVER) // 2 - 1)

        def chunk_view(s, a):
            return ring[:, s, :].rearrange("p (a n) -> p a n", a=a)

        @block.sync
        def _(sp):
            for j in range(J):
                src = x_prompt[0, j * P:(j + 1) * P, :] if j < J - 1 else x_sample.rearrange("b t d -> (b t) d")
                sp.dma_start(h[0:rows[j], j, :], src).then_inc(s_x[j], 16)
            win = w_in[0].rearrange("(k p) n -> p k n", p=P)
            for q in range(IN_CHUNKS):
                if q >= RING:
                    sp.wait_ge(s_win, q - RING + 1)
                for a in range(2):
                    col = (2 * q + a) * P if q < G // 2 else CH + (a * G + q - G // 2) * P
                    dst = ring[:, q % RING, a * K * P:(a + 1) * K * P].rearrange("p (k n) -> p k n", k=K)
                    sp.dma_start(dst, win[:, :, col:col + P]).then_inc(s_ring[q % RING], 16)
                if q == RING - 1:
                    sp.dma_start(poolw[:], pool_w[0].rearrange("g p n -> p g n")).then_inc(s_poolw, 16)
                    sp.dma_start(wout[:], w_out[0].rearrange("(k p) n -> p k n", p=P)).then_inc(s_wout, 16)

            sp.dma_start(router[:], w_router[0].rearrange("(k p) n -> p k n", p=P)).then_inc(s_router, 16)
            sp.dma_start(br[:], b_router.to_broadcast([P, E])).then_inc(s_router, 16)
            sp.dma_start(gmoe[:], g_moe.to_broadcast([P, D])).then_inc(s_gmoe, 16)
            sp.dma_start(pool_sample[0, :, 0:PB - NT, :], state_pool[0, :, NT:, :]).then_inc(s_cache, 16)
            sp.dma_start(conv_sample[0, :, 0:CB - NT, :], state_conv[0, :, NT:, :]).then_inc(s_cache, 16)

            def load(c0, it, src, a):
                if c0 >= RING:
                    sp.wait_ge(s_lo, c0 - RING + 1 + PER_LOOP * it)
                else:
                    sp.wait_ge(s_win, (5, 6, 3, 4)[c0])
                dst = chunk_view(c0 % RING, a) if a > 1 else ring[:, c0 % RING, :]
                sp.dma_start(dst, src).then_inc(s_ring[c0 % RING], 16)

            def load_gu(i0, it, e):
                w = w_gate_up[0, bass.ds(e, 1), :, :].rearrange("a (k p) n -> p (a k) n", p=P)
                for k in range(GU_CHUNKS):
                    load(gu_chunk(i0) + k, it, w[:, k, :], 1)

            def load_dn(i0, it, e, last=False):
                w = w_down[0, bass.ds(e, 1), :, :].rearrange("a (k p) n -> p (a k) n", p=P)
                for m in range(DN_CHUNKS):
                    load(dn_chunk(i0, last) + m, it, w[:, 2 * m:2 * m + 2, :], 2)

            load_gu(0, 0, 0)
            load_gu(1, 0, 1)
            load_dn(0, 0, 0)
            nit = n_loops(sp)
            with sp.Fori(0, nit) as it:
                e = [sp.value_load(blk_i[0:1, bass.ds(2 * it + n, 1)], min_val=0, max_val=E - 1) for n in (1, 2, 3)]
                for u in range(2):
                    load_gu(2 + u, it, e[u + 1])
                    load_dn(1 + u, it, e[u])
            e = sp.value_load(blk_i[0:1, bass.ds(2 * nit + 1, 1)], min_val=0, max_val=E - 1)
            load_dn(1, nit, e, last=True)
            sp.wait_ge(s_down, 2 + 2 * nit)
            sp.wait_ge(s_yst[0], 16 * (nit + 1))
            sp.wait_ge(s_yst[1], 16 * (nit + 1))
            for j in range(J):
                if j >= RING // 2:
                    sp.wait_ge(s_comb, TOP_K * (j - RING // 2 + 1))
                sp.dma_start(choices(j), rows_dram[j * P * TOP_K:(j * P + rows[j]) * TOP_K, :].rearrange("(p k) n -> p (k n)", k=TOP_K)
                             ).then_inc(s_gat[j], 16)

        @block.gpsimd
        def _(g):
            g.memset(ident[:], 0.0).then_inc(s_pad, 1)
            g.memset(before[:], 1.0).then_inc(s_pad, 1)
            g.memset(u_p[:, :, 0:PB], 0.0).then_inc(s_pad, 1)
            g.memset(glu_p[:, :, 0:CB], 0.0).then_inc(s_pad, 1)
            g.memset(ss[:], 1.0).then_inc(s_pad, 1)
            g.memset(mv[:], 1.0).then_inc(s_pad, 1)
            g.memset(L[:], 0.0).then_inc(s_pad, 1)
            g.memset(eps[:], RMS_EPS).then_inc(s_pad, 1)
            g.memset(ones[:], 1.0).then_inc(s_cst, 1)
            g.iota(iota_s[:], pattern=[[1, P]], base=0, channel_multiplier=0, allow_small_or_imprecise_dtypes=True).then_inc(s_cst, 1)
            g.iota(tokid[:], pattern=[[P, J]], base=0, channel_multiplier=1, allow_small_or_imprecise_dtypes=True).then_inc(s_cst, 1)
            g.iota(base1[:], pattern=[[P, E]], base=0, channel_multiplier=0, allow_small_or_imprecise_dtypes=True).then_inc(s_cst, 1)
            g.iota(part[:], pattern=[[0, 1]], base=0, channel_multiplier=1, allow_small_or_imprecise_dtypes=True).then_inc(s_cst, 1)
            g.iota(nth[:], pattern=[[1, TOP_K]], base=1, channel_multiplier=0, allow_small_or_imprecise_dtypes=True).then_inc(s_cst, 1)
            g.iota(inv[:], pattern=[[1, PB]], base=1, channel_multiplier=0, allow_small_or_imprecise_dtypes=True).then_inc(s_cst, 1)
            g.wait_ge(s_pad, 8)
            g.affine_select(out=ident[:], in_=ident[:], compare_op=ALU.not_equal, fill=1.0, base=0,
                            pattern=[[-1, P]], channel_multiplier=1).then_inc(s_cst, 1)
            g.affine_select(out=before[:], in_=before[:], compare_op=ALU.is_gt, fill=0.0, base=0,
                            pattern=[[1, P]], channel_multiplier=-1).then_inc(s_cst, 1)

            def gather(n0, it):
                n = n0 + 2 * it
                b = n0 % 2
                g.wait_ge(s_idx, n + 1)
                if n0 >= 2:
                    g.wait_ge(s_txd, n - 1)
                g.sem_inc(s_issued, 1)
                g.indirect_dma_start(row_buf[b][:, :], None, normed_dram[:, :],
                                     bass.IndirectOffsetOnAxis(ap=idx_cur[b][:, 0:1], axis=0),
                                     bounds_check=T - 1, oob_is_err=False).then_inc(s_xg[b], 16)

            def scatter(i0, it):
                i, b = i0 + 2 * it, i0 % 2
                g.wait_ge(s_row, i + 1)
                g.wait_ge(s_y, i + 1)
                g.sem_inc(s_issued, 1)
                g.indirect_dma_start(rows_dram[:, :], bass.IndirectOffsetOnAxis(ap=row_cur[b][:, 0:1], axis=0),
                                     y_sb[b][:, :], None, bounds_check=TOP_K * T - 1, oob_is_err=False).then_inc(s_yst[b], 16)

            for n, (src, own, ready) in enumerate(((u_s, PB, s_u), (glu_s, CB, s_glu))):
                g.wait_ge(ready, 2 * G)
                g.tensor_copy(newest[n].rearrange("p c (b t) -> p c b t", b=NB), src[:, :, :, own:]).then_inc(s_newest, 1)
            g.wait_ge(s_hrst[0], 16 * 3)
            g.wait_ge(s_hrst[1], 16 * 2)
            for n0 in range(4):
                gather(n0, 0)
            nit = n_loops(g)
            with g.Fori(0, nit) as it:
                for u in range(2):
                    scatter(u, it)
                    gather(4 + u, it)
            scatter(0, nit)
            scatter(1, nit)

        @block.scalar
        def _(act):
            for n, (v, a) in enumerate(((g_mix, 8), (g_moe, 8), (pool_scale, 4), (conv_b, 4), (conv_ln_g, 4), (conv_ln_b, 4))):
                r = (0, 8, 16, 20, 24, 28)[n]
                act.dma_start(vec_rows[r:r + a, :], v[0].rearrange("(k p) -> k p", p=P)).then_inc(s_vec, 16)
            act.dma_start(cw_rows, conv_w[0]).then_inc(s_state, 16)
            act.dma_start(sp_rows, state_pool[0].rearrange("b r c -> (b r) c")).then_inc(s_state, 16)
            for a in range(2):
                act.dma_start(sc_rows[:, a, :], state_conv[0, a * NB // 2:(a + 1) * NB // 2].rearrange("b r c -> (b r) c")).then_inc(s_state, 16)

            act.wait_ge(s_pad, 8)
            for j in range(J):
                act.wait_ge(s_x[j], 16)
                act.activation(out=junk[0:rows[j], :], in_=h[0:rows[j], j, :], func=ACT.Square,
                               accum_out=ss[0:rows[j], 0, j:j + 1]).then_inc(s_ss, 1)
                act.wait_ge(s_ss, j + 1)
            act.activation(out=ss[:, 1, :], in_=ss[:, 0, :], func=ACT.Sqrt, scale=1.0 / D, bias=eps[:]).then_inc(s_ss, 1)
            act.wait_ge(s_small, 5)
            for q in range(G // 2):
                act.wait_ge(s_proj, q + 1)
                for a in range(2):
                    g_ = 2 * q + a
                    b = 2 + 2 * (q % 2)
                    act.activation(out=u_p[:, g_, PB:], in_=ps[:, b + a, :], func=ACT.Copy).then_inc(s_u, 1)
                    act.activation(out=u_s[:, g_, :, PB:],
                                   in_=ps[:, 6 + q % 2, a * NS:(a + 1) * NS].rearrange("p (b t) -> p b t", b=NB),
                                   func=ACT.Copy).then_inc(s_u, 1)
            for q in range(G):
                act.wait_ge(s_proj, G // 2 + q + 1)
                if q >= 2:
                    act.wait_ge(s_glu, 2 * (q - 1))
                b = 2 + 2 * (q % 2)
                act.activation(out=sig_p[q % 2][:, 0:SEQ], in_=ps[:, b + 1, :], func=ACT.Sigmoid).then_inc(s_sig, 1)
                act.activation(out=sig_p[q % 2][:, SEQ:T], in_=ps[:, 6 + q % 2, NS:2 * NS], func=ACT.Sigmoid).then_inc(s_sig, 1)
            def tail(n, bank, r, dma):
                act.wait_ge(s_tail, n + 1)
                if n >= 2:
                    act.wait_ge(s_tout[n % 2], 16)
                act.activation(out=tails[n % 2][0:r, :], in_=ps[0:r, bank, :], func=ACT.Copy).then_inc(s_tailev, 1)
                act.wait_ge(s_tailev, n + 1)
                act.dma_start(dma, tails[n % 2][0:r, :]).then_inc(s_tout[n % 2], 16)
            act.wait_ge(s_tsmall, 1)
            tail(0, 0, PB, pool_prompt[0, 0])
            tail(1, 1, NS, pool_sample[0, :, PB - NT:, :])
            for g_ in range(G):
                act.wait_ge(s_pm, g_ + 1)
                act.activation(out=yT[:, g_, 0:SEQ], in_=ps[:, g_ % 2, :], func=ACT.Copy, scale=pscale[:, g_:g_ + 1]).then_inc(s_pool, 1)
            act.wait_ge(s_pm, G + 1)
            for g_ in range(G):
                act.activation(out=yT[:, g_, SEQ:T], in_=ps[:, 6, g_ * NS:(g_ + 1) * NS], func=ACT.Copy,
                               scale=pscale[:, g_:g_ + 1]).then_inc(s_pool, 1)
            for j in range(J):
                act.wait_ge(s_half, j + 1)
                act.activation(out=pool_out[j][0:rows[j], :], in_=ps[0:rows[j], 2 * (j % 2):2 * (j % 2) + 2, :].rearrange("p b n -> p (b n)"),
                               func=ACT.Copy).then_inc(s_halfev, 1)
            tail(2, 7, CB, conv_prompt[0, 0])
            tail(3, 0, NS, conv_sample[0, :, CB - NT:, :])
            act.wait_ge(s_var, J)
            act.activation(out=lnr[:, 0, :], in_=mv[:, :, 1], func=ACT.Sqrt, bias=eps[:]).then_inc(s_std, 1)
            for j in range(J):
                act.wait_ge(s_lnb, j + 1)
                for c in range(G):
                    act.activation(out=yT[:, G + c, j * P:j * P + rows[j]], in_=ps[:, 4 + j % 2, c * P:c * P + rows[j]],
                                   func=ACT.Silu, scale=lng[:, c:c + 1], bias=lnb[:, c:c + 1]).then_inc(s_conv, 1)
            for j in range(J):
                r = rows[j]
                act.wait_ge(s_h, J + j + 1)
                act.activation(out=junk[0:r, :], in_=h[0:r, j, :], func=ACT.Square,
                               accum_out=ss[0:r, 0, j:j + 1]).then_inc(s_ss2, 1)
                act.wait_ge(s_ss2, 2 * j + 1)
                act.activation(out=ss[0:r, 1, j:j + 1], in_=ss[0:r, 0, j:j + 1], func=ACT.Sqrt, scale=1.0 / D,
                               bias=eps[0:r, :]).then_inc(s_ss2, 1)
                act.wait_ge(s_hr, j + 1)
                act.dma_start(normed_dram[j * P:j * P + r, :], row_buf[j % 2][0:r, :]).then_inc(s_hrst[j % 2], 16)
                for half in range(2):
                    act.wait_ge(s_rt, 2 * j + half + 1)
                    act.activation(out=xT[j % 2][:, HALF * half:HALF * half + HALF, 0:r],
                                   in_=ps[:, half, :].rearrange("p (k t) -> p k t", k=HALF)[:, :, 0:r],
                                   func=ACT.Copy).then_inc(s_hnT, 1)
            for a in range(2):
                act.dma_start(bias_raw[a * E:(a + 1) * E, 0:2 * FF], b_gate_up[0]).then_inc(s_bias, 16)
                act.dma_start(bias_raw[a * E:(a + 1) * E, 2 * FF:], b_down[0]).then_inc(s_bias, 16)
            act.wait_ge(s_vs, 1)
            act.activation(out=gates[:], in_=dmod[:, 0], func=ACT.Exp).then_inc(s_exp, 1)

            def high(c0, it):
                act.wait_ge(s_ring[c0 % RING], landed(c0, it))
                if c0 >= RING:
                    act.wait_ge(s_used, c0 - RING + 1 + PER_LOOP * it)
                act.activation(out=w_hi[:, c0 % RING, :], in_=ring[:, c0 % RING, :], func=ACT.Copy).then_inc(s_hi, 1)

            def x_high(i0, it):
                act.wait_ge(s_txd, i0 + 1 + 2 * it)
                act.activation(out=x_hi[:].rearrange("p k t -> p (k t)"), in_=pst, func=ACT.Copy).then_inc(s_x_hi, 1)

            def h_high(i0, it):
                act.wait_ge(s_thd, i0 + 1 + 2 * it)
                act.activation(out=h_hi[:].rearrange("p k t -> p (k t)"), in_=pst, func=ACT.Copy, scale=1.0 / ALPHA).then_inc(s_h_hi, 1)

            def silu(i0, it):
                act.wait_ge(s_gs, i0 + 1 + 2 * it)
                act.activation(out=sig_s, in_=gate_s, func=ACT.Silu, scale=ALPHA).then_inc(s_act, 1)

            def result(i0, it):
                act.wait_ge(s_row, i0 + 1 + 2 * it)
                act.wait_ge(s_down, i0 + 1 + 2 * it)
                act.activation(out=y_sb[i0 % 2][:], in_=psd, func=ACT.Copy).then_inc(s_y, 1)

            def step(i0, it):
                for k in range(GU_CHUNKS):
                    high(gu_chunk(i0) + k, it)
                    if k == RING - 1:
                        if i0 >= 2:
                            result(i0 - 2, it)
                        if i0 >= 1:
                            h_high(i0 - 1, it)
                if i0 >= 1:
                    for m in range(DN_CHUNKS):
                        high(dn_chunk(i0 - 1) + m, it)
                x_high(i0 + 1, it)
                silu(i0, it)

            act.wait_ge(s_cache, 32)
            for n in range(2):
                act.wait_ge(s_tout[n], 32)
            act.wait_ge(s_bias, 64)
            act.activation(out=bias[:], in_=bias_raw, func=ACT.Copy).then_inc(s_biasp, 1)
            x_high(0, 0)
            step(0, 0)
            step(1, 0)
            nit = n_loops(act)
            with act.Fori(0, nit) as it:
                step(2, it)
                step(3, it)
            result(0, nit)
            h_high(1, nit)
            for m in range(DN_CHUNKS):
                high(dn_chunk(1, last=True) + m, nit)
            result(1, nit)
            act.dma_start(gfin[:], g_final.rearrange("(a n) -> a n", a=1).to_broadcast([P, D])).then_inc(s_gfin, 16)

            def store(j):
                act.wait_ge(s_fin, j + 1)
                dst = y_prompt[0, j * P:(j + 1) * P, :] if j < J - 1 else y_sample.rearrange("b t d -> (b t) d")
                act.dma_start(dst, h[0:rows[j], j, :]).then_inc(s_out, 16)

            for j in range(J):
                r = rows[j]
                act.wait_ge(s_comb, TOP_K * (j + 1))
                act.activation(out=gate_s[0:r, :], in_=h[0:r, j, :], func=ACT.Square,
                               accum_out=ss[0:r, 0, j:j + 1]).then_inc(s_ss3, 1)
                act.wait_ge(s_ss3, 2 * j + 1)
                act.activation(out=ss[0:r, 1, j:j + 1], in_=ss[0:r, 0, j:j + 1], func=ACT.Sqrt, scale=1.0 / D,
                               bias=eps[0:r, :]).then_inc(s_ss3, 1)
                if j:
                    store(j - 1)
            store(J - 1)
            act.wait_ge(s_out, 16 * J)

        @block.vector
        def _(dve):
            chain = [0]

            def link(ins):
                chain[0] += 1
                ins.then_inc(s_chain, 1)
                dve.wait_ge(s_chain, chain[0])

            dve.wait_ge(s_cst, 9)
            link(dve.reciprocal(inv[:], inv[:]))
            dve.wait_ge(s_tsmall, 1)
            dve.tensor_copy(vecT[:], ps[:, 6, 0:32]).then_inc(s_small, 1)
            dve.wait_ge(s_small, 1)
            dve.wait_ge(s_ss, J + 1)
            link(dve.reciprocal(ss[:, 2, :], ss[:, 1, :]))
            for j in range(J):
                dve.tensor_scalar(diag[:, j, :], ident[:], ss[:, 2, j:j + 1], None, ALU.mult).then_inc(s_xr, 1)

            def scaled(out, half, gT, r):
                return dve.tensor_tensor(out, ps[:, half, :].rearrange("p (k t) -> p k t", k=HALF)[:, :, 0:r],
                                         gT[:, HALF * half:HALF * half + HALF].unsqueeze(2).to_broadcast([P, HALF, r]), ALU.mult)

            for j in range(J):
                for half in range(2):
                    dve.wait_ge(s_tx, 2 * j + half + 1)
                    scaled(xnT[:, HALF * half:HALF * half + HALF, j * P:j * P + rows[j]], half, gmixT, rows[j]).then_inc(s_xnT, 1)

            dve.wait_ge(s_tsmall, 2)
            dve.tensor_copy(cwT[:].rearrange("p c t -> p (c t)"), ps[:, 6, 32:32 + G * TAPS]).then_inc(s_small, 1)
            dve.tensor_copy(u_s[:, :, :, 0:PB], ps[:, 4, 0:G * NB * PB].rearrange("p (c b r) -> p c b r", c=G, b=NB)).then_inc(s_small, 1)
            for a in range(2):
                dve.tensor_copy(glu_s[:, :, a * NB // 2:(a + 1) * NB // 2, 0:CB],
                                ps[:, 5 + 2 * a, 0:G * NB // 2 * CB].rearrange("p (c b r) -> p c b r", c=G, b=NB // 2)).then_inc(s_small, 1)
            dve.wait_ge(s_small, 5)

            dve.wait_ge(s_pad, 8)
            for g_, w in enumerate(WINDOWS):
                dve.wait_ge(s_u, 2 * g_ + 2)
                src_p, src_s = u_p[:, g_, :], u_s[:, g_, :, :]
                for m in range(g_ + 1):
                    lo, sh = 2 ** (m + 1) - 1, 2 ** m
                    dve.tensor_tensor(win_s[m % 2][:, :, lo:], src_s[:, :, lo:], src_s[:, :, lo - sh:PB + NT - sh], ALU.add)
                    link(dve.tensor_tensor(win_p[m % 2][:, lo:], src_p[:, lo:], src_p[:, lo - sh:PB + SEQ - sh], ALU.add))
                    src_p, src_s = win_p[m % 2][:, :], win_s[m % 2][:, :, :]
                dve.scalar_tensor_tensor(out=z[:, g_, SEQ:T].rearrange("p (b t) -> p b t", b=NB), in0=src_s[:, :, PB:], scalar=1.0 / w,
                                         in1=u_s[:, g_, :, PB:], op0=ALU.mult, op1=ALU.subtract)
                dve.tensor_tensor(fix[:, 0:w - 1], src_p[:, PB:PB + w - 1], inv[:, 0:w - 1], ALU.mult)
                link(dve.scalar_tensor_tensor(out=z[:, g_, 0:SEQ], in0=src_p[:, PB:], scalar=1.0 / w, in1=u_p[:, g_, PB:],
                                              op0=ALU.mult, op1=ALU.subtract))
                dve.tensor_tensor(z[:, g_, 0:w - 1], fix[:, 0:w - 1], u_p[:, g_, PB:PB + w - 1], ALU.subtract).then_inc(s_z, 1)
                dve.wait_ge(s_z, g_ + 1)

            odd_p = win_p[0][:, 0:SEQ]
            with dve.Fori(0, G // 2) as it:
                for n in range(2):
                    q = 2 * it + n
                    b = 2 + 2 * n
                    dve.wait_ge(s_sig, 4 * it + 2 * n + 2)
                    dve.tensor_tensor(glu_p[:, bass.ds(q, 1), CB:].rearrange("p a t -> p (a t)"), ps[:, b, :],
                                      sig_p[n][:, 0:SEQ], ALU.mult).then_inc(s_glu, 1)
                    dve.tensor_tensor(glu_s[:, bass.ds(q, 1), :, CB:].rearrange("p a b t -> p (a b) t"),
                                      ps[:, 6 + n, 0:NS].rearrange("p (b t) -> p b t", b=NB),
                                      sig_p[n][:, SEQ:T].rearrange("p (b t) -> p b t", b=NB), ALU.mult).then_inc(s_glu, 1)
                    dve.wait_ge(s_glu, 4 * it + 2 * n + 2)
                    acc_p = conv[:, bass.ds(q, 1), 0:SEQ].rearrange("p a t -> p (a t)")
                    acc_s = conv[:, bass.ds(q, 1), SEQ:T].rearrange("p a (b t) -> p (a b) t", b=NB)
                    for t in range(TAPS):
                        w = cwT[:, bass.ds(q, 1), t:t + 1].rearrange("p a t -> p (a t)")
                        src_p = glu_p[:, bass.ds(q, 1), t:t + SEQ].rearrange("p a t -> p (a t)")
                        src_s = glu_s[:, bass.ds(q, 1), :, t:t + NT].rearrange("p a b t -> p (a b) t")
                        if t == 0:
                            cb = convb[:, bass.ds(q, 1)]
                            dve.tensor_scalar(acc_p, src_p, w, cb, ALU.mult, ALU.add).then_inc(s_convp, 1)
                            dve.tensor_scalar(acc_s, src_s, w, cb, ALU.mult, ALU.add).then_inc(s_convs, 1)
                        else:
                            if t == 1:
                                dve.tensor_scalar(odd_p, src_p, w, None, ALU.mult).then_inc(s_convp, 1)
                            else:
                                dve.wait_ge(s_convp, 2 * (TAPS + 1) * it + (TAPS + 1) * n + t - 1)
                                acc = odd_p if t % 2 else acc_p
                                dve.scalar_tensor_tensor(out=acc, in0=src_p, scalar=w, in1=acc, op0=ALU.mult, op1=ALU.add).then_inc(s_convp, 1)
                            dve.wait_ge(s_convs, 2 * TAPS * it + TAPS * n + t)
                            dve.scalar_tensor_tensor(out=acc_s, in0=src_s, scalar=w, in1=acc_s, op0=ALU.mult, op1=ALU.add).then_inc(s_convs, 1)
                    dve.wait_ge(s_convp, 2 * (TAPS + 1) * it + (TAPS + 1) * n + TAPS)
                    dve.tensor_tensor(acc_p, acc_p, odd_p, ALU.add).then_inc(s_convp, 1)

            for j in range(J):
                r, bank = rows[j], (0, 1, 2, 3, 6)[j]
                dve.wait_ge(s_lnf, j + 1)
                link(dve.bn_stats(st[0:r, :], ps[0:r, bank, :]))
                dve.bn_aggr(mv[0:r, j, :], st[0:r, :]).then_inc(s_var, 1)
                dve.wait_ge(s_var, j + 1)
            dve.wait_ge(s_std, 1)
            link(dve.reciprocal(lnr[:, 1, :], lnr[:, 0, :]))
            for j in range(J):
                r, bank = rows[j], (0, 1, 2, 3, 6)[j]
                if j >= 2:
                    dve.wait_ge(s_lnb, j - 1)
                dve.tensor_scalar(sig_p[j % 2][0:r, 0:CH], ps[0:r, bank, :], mv[0:r, j, 0:1], lnr[0:r, 1, j:j + 1],
                                  ALU.subtract, ALU.mult).then_inc(s_nrm, 1)
            for j in range(J):
                r = rows[j]
                dve.wait_ge(s_halfev, j + 1)
                dve.tensor_tensor(h[0:r, j, :], h[0:r, j, :], pool_out[j][0:r, :], ALU.add).then_inc(s_h, 1)

            dve.wait_ge(s_gmoe, 16)
            def topk(j):
                r = rows[j]
                dve.wait_ge(s_log, j + 1)
                dve.tensor_tensor(L[0:r, j, :], ps[0:r, 4, j * E:(j + 1) * E], br[0:r, :], ALU.add).then_inc(s_L, 1)
                dve.wait_ge(s_L, j + 1)
                link(dve.max(v8[:, j, :], L[:, j, :]))
                link(dve.max_index(i8[:, j, :], v8[:, j, :], L[:, j, :]))

            dve.wait_ge(s_router, 32)
            for j in range(J):
                r, b = rows[j], 6 - 4 * (j % 2)
                dve.wait_ge(s_op, j + 1)
                dve.wait_ge(s_h, J + j)
                dve.tensor_tensor(h[0:r, j, :], h[0:r, j, :], ps[0:r, b:b + 2, :].rearrange("p b n -> p (b n)"), ALU.add).then_inc(s_h, 1)
                dve.wait_ge(s_ss2, 2 * j + 2)
                link(dve.reciprocal(ss[0:r, 3, j:j + 1], ss[0:r, 1, j:j + 1]))
                if j >= 2:
                    dve.wait_ge(s_rt, 2 * (j - 1))
                    dve.wait_ge(s_hrst[j % 2], 16 * (j // 2))
                dve.scalar_tensor_tensor(out=row_buf[j % 2][0:r, :], in0=h[0:r, j, :], scalar=ss[0:r, 3, j:j + 1],
                                         in1=gmoe[0:r, :], op0=ALU.mult, op1=ALU.mult).then_inc(s_hr, 1)
                if j >= 1:
                    topk(j - 1)
            topk(J - 1)

            dve.tensor_tensor(dmod[:, 0], v8[:, :, 0:TOP_K], v8[:, :, 0:1].to_broadcast([P, J, TOP_K]), ALU.subtract).then_inc(s_vs, 1)
            link(dve.tensor_copy(idxf[:], i8[:, :, 0:TOP_K]))
            for j in range(J):
                last = dve.tensor_tensor(oh[:, j], iota_s[:, 0:E].unsqueeze(1).to_broadcast([P, TOP_K, E]),
                                         idxf[:, j, :].unsqueeze(2).to_broadcast([P, TOP_K, E]), ALU.is_equal)
            link(last)
            with nc.allow_low_precision(reason="sums of at most one 1"):
                for j in range(J):
                    last = dve.tensor_reduce(mask[:, j, :], oh[:, j].rearrange("p k e -> p e k"), AX.X, ALU.add)
                last.then_inc(s_mask, 1)
            dve.wait_ge(s_exp, 1)
            link(dve.tensor_reduce(gsum[:, 0, :], gates[:], AX.X, ALU.add))
            link(dve.reciprocal(gsum[:, 1, :], gsum[:, 0, :]))
            link(dve.tensor_tensor(gates[:], gates[:], gsum[:, 1, :].unsqueeze(2).to_broadcast([P, J, TOP_K]), ALU.mult))

            dve.wait_ge(s_rank, 1)
            cnt = ps[:, 5, J * E:(J + 1) * E]
            link(dve.tensor_scalar(over[:, 0, :], cnt, float(P), None, ALU.is_gt))
            for b in range(2, J):
                link(dve.scalar_tensor_tensor(out=over[:, 0, :], in0=cnt, scalar=float(b * P), in1=over[:, 0, :],
                                              op0=ALU.is_gt, op1=ALU.add))
            link(dve.tensor_copy(over[:, 1, :], over[:, 0, :]))
            src, sh = 1, 1
            while sh < E:
                dst = 3 - src
                dve.tensor_copy(over[:, dst, 0:sh], over[:, src, 0:sh])
                link(dve.tensor_tensor(over[:, dst, sh:], over[:, src, sh:], over[:, src, 0:E - sh], ALU.add))
                src, sh = dst, 2 * sh
            total = over[:, src, :]
            link(dve.tensor_tensor(over[:, 3, :], total, over[:, 0, :], ALU.subtract))
            link(dve.tensor_scalar(over[:, 3, :], over[:, 3, :], float(P), float(P * (E - 1)), ALU.mult, ALU.add))
            link(dve.tensor_tensor(over[:, 4, :], over[:, 3, :], base1[:], ALU.subtract))
            for j in range(J):
                rank = ps[:, 5, j * E:(j + 1) * E]
                link(dve.scalar_tensor_tensor(out=dest[:, j, :], in0=rank, scalar=float(P), in1=over[:, 4, :],
                                              op0=ALU.is_ge, op1=ALU.mult))
                link(dve.tensor_tensor(dest[:, j, :], dest[:, j, :], rank, ALU.add))
                link(dve.tensor_tensor(dest[:, j, :], dest[:, j, :], base1[:], ALU.add))
                link(dve.tensor_tensor(oh[:, j], oh[:, j], dest[:, j, :].unsqueeze(1).to_broadcast([P, TOP_K, E]), ALU.mult))
                link(dve.tensor_reduce(dest4[:, j, :], oh[:, j], AX.X, ALU.add))
            link(dve.tensor_copy(desti[:, 0], dest4[:]))
            dve.tensor_scalar(desti[:, 1], desti[:, 0], 7, None, ALU.arith_shift_right)
            link(dve.tensor_scalar(desti[:, 2], desti[:, 0], P - 1, None, ALU.bitwise_and))
            dve.tensor_copy(dmod[:, 1], desti[:, 1])
            link(dve.tensor_copy(dmod[:, 0], desti[:, 2]))
            for j in range(J):
                if j:
                    dve.wait_ge(s_inv, j)
                dve.tensor_tensor(inA, iota_s[:].unsqueeze(1).to_broadcast([P, TOP_K, P]),
                                  dmod[:, 0, j, :].unsqueeze(2).to_broadcast([P, TOP_K, P]), ALU.is_equal)
                link(dve.tensor_tensor(inB[:, :, 0, :], iota_s[:, 0:COLS].unsqueeze(1).to_broadcast([P, TOP_K, COLS]),
                                       dmod[:, 1, j, :].unsqueeze(2).to_broadcast([P, TOP_K, COLS]), ALU.is_equal))
                link(dve.tensor_tensor(inB[:, :, 1, :], inB[:, :, 0, :], nth[:].unsqueeze(2).to_broadcast([P, TOP_K, COLS]), ALU.mult))
                dve.tensor_scalar(inB[:, :, 0, :], inB[:, :, 0, :], tokid[:, j:j + 1], None, ALU.mult).then_inc(s_ab, 1)
            dve.tensor_copy(blk_e[:, 0:E], iota_s[:, 0:E])
            link(dve.tensor_tensor(cmp[:], iota_s[:, 0:COLS - E].unsqueeze(2).to_broadcast([P, COLS - E, E]),
                                   total.unsqueeze(1).to_broadcast([P, COLS - E, E]), ALU.is_ge))
            link(dve.tensor_reduce(blk_e[:, E:], cmp[:], AX.X, ALU.add))
            link(dve.tensor_scalar(blk_e[:, E:], blk_e[:, E:], float(E - 1), None, ALU.min))
            link(dve.tensor_scalar(low[:], part[:], float(E), float(-E), ALU.is_ge, ALU.mult))
            link(dve.tensor_tensor(low[:], low[:], part[:], ALU.add))
            link(dve.tensor_scalar(selm[:], blk_e[0:2 * E, :], low[:], None, ALU.is_equal))
            dve.tensor_copy(blk_i[:], blk_e[0:1, :]).then_inc(s_tab, 1)
            link(dve.tensor_scalar(nit_f[:, 0:1], total[:, E - 1:E], float(E - 1), None, ALU.add))
            link(dve.tensor_copy(nit_i[:, 0:1], nit_f[:, 0:1]))
            dve.tensor_scalar(nit_i[:, 1:2], nit_i[:, 0:1], 1, None, ALU.arith_shift_right).then_inc(s_tab, 1)
            dve.wait_ge(s_inv, J)
            choice = ps[:, 4, J * E + COLS:J * E + 2 * COLS]
            link(dve.tensor_scalar(none[:], choice, 0.0, float(NO_ROW), ALU.is_equal, ALU.mult))
            link(dve.tensor_tensor(tok_f[:], ps[:, 4, J * E:J * E + COLS], none[:], ALU.add))
            link(dve.tensor_copy(slot_tok[:], tok_f[:]))
            link(dve.tensor_scalar(tok_f[:], tok_f[:], float(TOP_K), -1.0, ALU.mult, ALU.add))
            link(dve.tensor_tensor(slot_row[:], tok_f[:], choice, ALU.add))

            def tokens(i0, it):
                b = i0 % 2
                if i0 >= 2:
                    dve.wait_ge(s_xg[b], 16 * (i0 // 2) + 16 * it)
                dve.tensor_copy(idx_cur[b][:], slot_tok[:, bass.ds(i0 + 2 * it, 1)]).then_inc(s_idx, 1)

            def places(i0, it):
                b = i0 % 2
                if i0 >= 2:
                    dve.wait_ge(s_yst[b], 16 * (i0 // 2) + 16 * it)
                dve.tensor_copy(row_cur[b][:], slot_row[:, bass.ds(i0 + 2 * it, 1)]).then_inc(s_row, 1)

            def select(i0, it):
                if i0 >= 2:
                    dve.wait_ge(s_dsel, i0 - 1 + 2 * it)
                dve.tensor_copy(sel_cur[i0 % 2][:], selm[:, bass.ds(i0 + 2 * it, 1)].to_broadcast([2 * E, P])).then_inc(s_sel, 1)

            def low_part(c0, it):
                dve.wait_ge(s_hi, c0 + 1 + PER_LOOP * it)
                dve.tensor_tensor(w_lo[:, c0 % RING, :], ring[:, c0 % RING, :], w_hi[:, c0 % RING, :].bitcast(F32),
                                  ALU.subtract).then_inc(s_lo, 1)

            def x_low(i0, it):
                dve.wait_ge(s_x_hi, i0 + 1 + 2 * it)
                dve.tensor_tensor(x_lo[:].rearrange("p k t -> p (k t)"), pst, x_hi[:].bitcast(F32).rearrange("p k t -> p (k t)"),
                                  ALU.subtract).then_inc(s_x_lo, 1)

            def h_low(i0, it):
                dve.wait_ge(s_h_hi, i0 + 1 + 2 * it)
                dve.scalar_tensor_tensor(out=h_lo[:].rearrange("p k t -> p (k t)"), in0=pst, scalar=1.0 / ALPHA,
                                         in1=h_hi[:].bitcast(F32).rearrange("p k t -> p (k t)"),
                                         op0=ALU.mult, op1=ALU.subtract).then_inc(s_h_lo, 1)

            def swiglu(i0, it):
                i = i0 + 2 * it
                dve.wait_ge(s_gu, i + 1)
                dve.tensor_scalar(gate_s, psg, LIMIT, None, ALU.min).then_inc(s_gs, 1)
                dve.tensor_scalar(up_s, psu, LIMIT, -LIMIT, ALU.min, ALU.max).then_inc(s_free, 1)
                dve.wait_ge(s_free, i + 1)
                dve.wait_ge(s_act, i + 1)
                dve.scalar_tensor_tensor(out=up_s, in0=up_s, scalar=1.0, in1=sig_s, op0=ALU.add, op1=ALU.mult).then_inc(s_hdn, 1)

            def step(i0, it):
                tokens(i0 + 2, it)
                for k in range(GU_CHUNKS):
                    low_part(gu_chunk(i0) + k, it)
                    if k == RING - 1 and i0 >= 1:
                        h_low(i0 - 1, it)
                if i0 >= 1:
                    for m in range(DN_CHUNKS):
                        low_part(dn_chunk(i0 - 1) + m, it)
                swiglu(i0, it)
                x_low(i0 + 1, it)
                select(i0 + 1, it)
                places(i0, it)

            tokens(0, 0)
            tokens(1, 0)
            select(0, 0)
            dve.wait_ge(s_biasp, 1)
            dve.tensor_tensor(bias[E:2 * E, :], bias_raw[E:2 * E, :], bias[E:2 * E, :].bitcast(F32), ALU.subtract).then_inc(s_biasp, 1)
            x_low(0, 0)
            step(0, 0)
            step(1, 0)
            nit = n_loops(dve)
            with dve.Fori(0, nit) as it:
                step(2, it)
                step(3, it)
            h_low(1, nit)
            for m in range(DN_CHUNKS):
                low_part(dn_chunk(1, last=True) + m, nit)

            dve.wait_ge(s_gfin, 16)

            def normed(j):
                r = rows[j]
                dve.wait_ge(s_ss3, 2 * j + 2)
                link(dve.reciprocal(ss[0:r, 2, j:j + 1], ss[0:r, 1, j:j + 1]))
                dve.scalar_tensor_tensor(out=h[0:r, j, :], in0=h[0:r, j, :], scalar=ss[0:r, 2, j:j + 1], in1=gfin[0:r, :],
                                         op0=ALU.mult, op1=ALU.mult).then_inc(s_fin, 1)

            for j in range(J):
                r = rows[j]
                dve.wait_ge(s_gat[j], 16)
                for k in range(TOP_K):
                    if k:
                        dve.wait_ge(s_comb, j * TOP_K + k)
                    dve.scalar_tensor_tensor(out=h[0:r, j, :], in0=choices(j)[:, k * D:(k + 1) * D], scalar=gates[0:r, j, k:k + 1],
                                             in1=h[0:r, j, :], op0=ALU.mult, op1=ALU.add).then_inc(s_comb, 1)
                if j:
                    normed(j - 1)
            normed(J - 1)

        @block.tensor
        def _(pe):
            pe.wait_ge(s_cst, 9)
            pe.wait_ge(s_vec, 16 * 6)
            pe.transpose(ps[:, 6, 0:32], vec_rows[:], ident[0:32, 0:32]).then_inc(s_tsmall, 1)

            def turn(src, r, first, ready, done):
                for half in range(2):
                    if first is not None:
                        pe.wait_ge(ready, first + half)
                    for m in range(HALF):
                        k = HALF * half + m
                        last = pe.transpose(ps[:, half, m * P:m * P + r], src[0:r, k * P:(k + 1) * P], ident[0:r, 0:r])
                    last.then_inc(done, 1)

            for j in range(J):
                r = rows[j]
                pe.wait_ge(s_xr, j + 1)
                for half in range(2):
                    if j:
                        pe.wait_ge(s_xnT, 2 * j - 1 + half)
                    for m in range(HALF):
                        k = HALF * half + m
                        last = pe.matmul(ps[:, half, m * P:m * P + r], lhsT=h[0:r, j, k * P:(k + 1) * P], rhs=diag[0:r, j, 0:r],
                                         start=True, stop=True)
                    last.then_inc(s_tx, 1)

            pe.wait_ge(s_state, 16 * 4)
            pe.wait_ge(s_small, 1)
            for c in range(G):
                pe.transpose(ps[:, 6, 32 + c * TAPS:32 + (c + 1) * TAPS], cw_rows[:, c * P:(c + 1) * P], ident[0:TAPS, 0:TAPS])
                n = NB * PB
                pe.transpose(ps[:, 4, c * n:(c + 1) * n], sp_rows[:, c * P:(c + 1) * P], ident[0:n, 0:n])
                n = NB // 2 * CB
                for a in range(2):
                    last = pe.transpose(ps[:, 5 + 2 * a, c * n:(c + 1) * n], sc_rows[:, a, c * P:(c + 1) * P], ident[0:n, 0:n])
            last.then_inc(s_tsmall, 1)
            pe.wait_ge(s_xnT, 2 * J)

            for q in range(IN_CHUNKS):
                pe.wait_ge(s_ring[q % RING], 32 * (q // RING + 1))
                b = 2 + 2 * (q % 2)
                if q < 2:
                    pe.wait_ge(s_small, (2, 5)[q])
                elif q < 4:
                    pe.wait_ge(s_u, 4 * (q - 1))
                else:
                    pe.wait_ge(s_glu, 2 * (q - 3))
                for a in range(2):
                    w = ring[:, q % RING, a * K * P:(a + 1) * K * P].rearrange("p (k n) -> p k n", k=K)
                    for k in range(K):
                        pe.matmul(ps[:, b + a, :], lhsT=w[:, k, :], rhs=xnT[:, k, 0:SEQ], start=k == 0, stop=k == K - 1)
                    for k in range(K):
                        last = pe.matmul(ps[:, 6 + q % 2, a * NS:(a + 1) * NS], lhsT=w[:, k, :], rhs=xnT[:, k, SEQ:T],
                                         start=k == 0, stop=k == K - 1)
                last.then_inc(s_proj, 1)
                pe.wait_ge(s_proj, q + 1)
                pe.sem_inc(s_win, 1)

            pe.wait_ge(s_u, 2 * G)
            def tails_of(src, r, bank):
                for c in range(G):
                    last = pe.transpose(ps[0:r, bank, c * P:(c + 1) * P], src(c), ident[:])
                last.then_inc(s_tail, 1)
            tails_of(lambda c: u_p[:, c, PB + SEQ - PB:], PB, 0)
            pe.wait_ge(s_newest, 1)
            tails_of(lambda c: newest[0][:, c, :], NS, 1)
            pe.wait_ge(s_poolw, 16)
            pe.wait_ge(s_z, G)
            pe.wait_ge(s_tailev, 2)
            for g_ in range(G):
                if g_ >= 2:
                    pe.wait_ge(s_pool, g_ - 1)
                pe.matmul(ps[:, g_ % 2, :], lhsT=poolw[:, g_, :], rhs=z[:, g_, 0:SEQ], start=True, stop=True).then_inc(s_pm, 1)
            pe.wait_ge(s_glu, 2 * (G - 1))
            for g_ in range(G):
                last = pe.matmul(ps[:, 6, g_ * NS:(g_ + 1) * NS], lhsT=poolw[:, g_, :], rhs=z[:, g_, SEQ:T],
                                 start=True, stop=True)
            last.then_inc(s_pm, 1)

            def output(j, b, k0, done):
                r = rows[j]
                for k in range(k0, k0 + G):
                    for n in range(2):
                        last = pe.matmul(ps[0:r, b + n, :], lhsT=yT[:, k, j * P:j * P + r], rhs=wout[:, k, n * 512:(n + 1) * 512],
                                         start=k == k0, stop=k == k0 + G - 1)
                last.then_inc(done, 1)

            pe.wait_ge(s_wout, 16)
            pe.wait_ge(s_pool, 2 * G)
            for j in range(J):
                if j >= 2:
                    pe.wait_ge(s_halfev, j - 1)
                output(j, 2 * (j % 2), 0, s_half)
            pe.wait_ge(s_glu, 2 * G)
            tails_of(lambda c: glu_p[:, c, CB + SEQ - CB:], CB, 7)
            pe.wait_ge(s_newest, 2)
            pe.wait_ge(s_halfev, J)
            tails_of(lambda c: newest[1][:, c, :], NS, 0)

            pe.wait_ge(s_convp, (TAPS + 1) * G)
            pe.wait_ge(s_convs, TAPS * G)
            pe.wait_ge(s_tailev, 4)
            for j in range(J):
                bank = (0, 1, 2, 3, 6)[j]
                for c in range(G):
                    last = pe.transpose(ps[0:rows[j], bank, c * P:(c + 1) * P], conv[:, c, j * P:j * P + rows[j]], ident[:])
                last.then_inc(s_lnf, 1)
            for j in range(J):
                r = rows[j]
                pe.wait_ge(s_nrm, j + 1)
                if j >= 2:
                    pe.wait_ge(s_conv, G * (j - 1))
                for c in range(G):
                    last = pe.transpose(ps[:, 4 + j % 2, c * P:c * P + r], sig_p[j % 2][0:r, c * P:(c + 1) * P], ident[0:r, 0:r])
                last.then_inc(s_lnb, 1)

            def conv_half(j):
                pe.wait_ge(s_conv, G * (j + 1))
                if j >= 2:
                    pe.wait_ge(s_h, J + j - 1)
                output(j, 6 - 4 * (j % 2), G, s_op)

            def logits(j):
                r = rows[j]
                pe.wait_ge(s_hr, j + 1)
                turn(row_buf[j % 2], r, 2 * j - 1 if j else None, s_hnT, s_rt)
                pe.wait_ge(s_hnT, 2 * j + 2)
                if j:
                    pe.wait_ge(s_L, j)
                for k in range(K):
                    last = pe.matmul(ps[0:r, 4, j * E:(j + 1) * E], lhsT=xT[j % 2][:, k, 0:r], rhs=router[:, k, :],
                                     start=k == 0, stop=k == K - 1)
                last.then_inc(s_log, 1)

            pe.wait_ge(s_router, 32)
            pe.wait_ge(s_nrm, J)
            conv_half(0)
            conv_half(1)
            pe.wait_ge(s_conv, G * J)
            for j in range(J):
                logits(j)
                if j + 2 < J:
                    conv_half(j + 2)

            pe.wait_ge(s_mask, 1)
            for j in range(J):
                for i in range(j):
                    pe.matmul(ps[:, 5, j * E:(j + 1) * E], lhsT=ones[:], rhs=mask[:, i, :], start=i == 0, stop=False)
                r = rows[j]
                pe.matmul(ps[:, 5, j * E:(j + 1) * E], lhsT=before[0:r, :], rhs=mask[0:r, j, :], start=j == 0, stop=True)
            for j in range(J):
                r = rows[j]
                last = pe.matmul(ps[:, 5, J * E:(J + 1) * E], lhsT=ones[0:r, :], rhs=mask[0:r, j, :], start=j == 0, stop=j == J - 1)
            last.then_inc(s_rank, 1)
            for j in range(J):
                r = rows[j]
                pe.wait_ge(s_ab, j + 1)
                for k in range(TOP_K):
                    last = pe.matmul(ps[:, 4, J * E:J * E + 2 * COLS], lhsT=inA[0:r, k, :], rhs=inB[0:r, k, :, :],
                                     start=j == 0 and k == 0, stop=j == J - 1 and k == TOP_K - 1)
                last.then_inc(s_inv, 1)

            def turn_x(i0, it):
                i, b = i0 + 2 * it, i0 % 2
                pe.wait_ge(s_xg[b], 16 * (i0 // 2 + 1) + 16 * it)
                if i0 >= 2:
                    pe.wait_ge(s_h_lo, i - 1)
                for k in range(K):
                    last = pe.transpose(ps[:, k // HALF, k % HALF * P:(k % HALF + 1) * P], row_buf[b][:, k * P:(k + 1) * P], ident[:])
                last.then_inc(s_txd, 1)

            def turn_h(i0, it):
                i = i0 + 2 * it
                pe.wait_ge(s_hdn, i + 1)
                pe.wait_ge(s_x_lo, i + 2)
                for k in range(KF):
                    last = pe.transpose(ps[:, k // HALF, k % HALF * P:(k % HALF + 1) * P], up_s[:, k * P:(k + 1) * P], ident[:])
                last.then_inc(s_thd, 1)

            def product(banks, hi, lo, whi, wlo, stop):
                for lhs, w in ((hi, whi), (hi, wlo), (lo, whi)):
                    for n in range(banks.shape[1]):
                        last = pe.matmul(banks[:, n, :], lhsT=lhs, rhs=w[:, n * 512:(n + 1) * 512], start=False,
                                         stop=stop and lhs is lo)
                return last

            def gate_up(i0, it):
                i, b = i0 + 2 * it, i0 % 2
                pe.wait_ge(s_x_lo, i + 1)
                pe.wait_ge(s_sel, i + 1)
                if i0:
                    pe.wait_ge(s_free, i)
                for n in range(4):
                    pe.matmul(ps[:, 4 + n, :], lhsT=sel_cur[b][:], rhs=bias[:, n * 512:(n + 1) * 512], start=True, stop=False)
                for k in range(K):
                    c = gu_chunk(i0) + k
                    pe.wait_ge(s_lo, c + 1 + PER_LOOP * it)
                    last = product(ps[:, 4:8, :], x_hi[:, k, :], x_lo[:, k, :], w_hi[:, c % RING, :], w_lo[:, c % RING, :], k == K - 1)
                    last.then_inc(s_used if k < K - 1 else s_gu, 1)
                pe.wait_ge(s_gu, i + 1)
                pe.sem_inc(s_used, 1)

            def down(i0, it, last_block=False):
                i, b = i0 + 2 * it, i0 % 2
                pe.wait_ge(s_h_lo, i + 1)
                if i0:
                    pe.wait_ge(s_y, i)
                for n in range(2):
                    last = pe.matmul(ps[:, 2 + n, :], lhsT=sel_cur[b][:], rhs=bias[:, 2 * FF + n * 512:2 * FF + (n + 1) * 512],
                                     start=True, stop=False)
                last.then_inc(s_dsel, 1)
                for k in range(KF):
                    c = dn_chunk(i0, last_block) + k // 2
                    if k % 2 == 0:
                        pe.wait_ge(s_lo, c + 1 + PER_LOOP * it)
                    part_of = slice(k % 2 * D, (k % 2 + 1) * D)
                    last = product(ps[:, 2:4, :], h_hi[:, k, :], h_lo[:, k, :], w_hi[:, c % RING, part_of], w_lo[:, c % RING, part_of], k == KF - 1)
                    if k % 2:
                        last.then_inc(s_used if k < KF - 1 else s_down, 1)
                pe.wait_ge(s_down, i + 1)
                pe.sem_inc(s_used, 1)

            pe.wait_ge(s_biasp, 2)
            turn_x(0, 0)
            gate_up(0, 0)
            turn_x(1, 0)
            turn_h(0, 0)
            gate_up(1, 0)
            turn_x(2, 0)
            down(0, 0)
            turn_h(1, 0)
            nit = n_loops(pe)
            with pe.Fori(0, nit) as it:
                for u in range(2):
                    gate_up(2 + u, it)
                    turn_x(3 + u, it)
                    down(1 + u, it)
                    turn_h(2 + u, it)
            down(1, nit, last_block=True)


_INS = ["x_prompt", "x_sample", "state_pool", "state_conv", "g_mix", "w_in", "pool_w", "pool_scale", "conv_w", "conv_b",
        "conv_ln_g", "conv_ln_b", "w_out", "g_moe", "w_router", "b_router", "w_gate_up", "b_gate_up", "w_down", "b_down",
        "g_final"]
_OUTS = [(1, 512, 1024), (8, 8, 1024), (1, 1, 15, 512), (1, 1, 30, 512), (1, 8, 15, 512), (1, 8, 30, 512)]


def kernel(**inputs):
    import numpy as _np
    import concourse.bacc as _bacc
    from concourse import mybir as _mybir
    from concourse.bass_utils import run_bass_kernel_spmd as _run

    nc = _bacc.Bacc("TRN2", target_bir_lowering=False, num_devices=1)
    arrays, args = {}, []
    for name in _INS:
        a = _np.ascontiguousarray(inputs[name])
        arrays[f"in_{name}_dram"] = a
        args.append(nc.dram_tensor(f"in_{name}_dram", a.shape, _mybir.dt.from_np(a.dtype), kind="ExternalInput").ap())
    for i, shape in enumerate(_OUTS):
        args.append(nc.dram_tensor(f"out_{i}_dram", shape, _mybir.dt.float32, kind="ExternalOutput").ap())
    args.append(nc.dram_tensor("normed_rows_dram", (576, 1024), _mybir.dt.float32, kind="Internal").ap())
    args.append(nc.dram_tensor("choice_rows_dram", (576 * 4, 1024), _mybir.dt.float32, kind="Internal").ap())
    hybrid_moe_step(nc, *args)
    r = _run(nc, [arrays], core_ids=[0])
    return tuple(r.results[0][f"out_{i}_dram"] for i in range(len(_OUTS)))
```

```python
from contextlib import ExitStack

import concourse.bass as bass
from concourse import mybir

P = 128
F32 = mybir.dt.float32
F32R = mybir.dt.float32r
F16 = mybir.dt.float16
I32 = mybir.dt.int32
U32 = mybir.dt.uint32
ALU = mybir.AluOpType
ACT = mybir.ActivationFunctionType
AX = mybir.AxisListType

WINDOWS = (2, 4, 8, 16)
TOP_K = 4
RMS_EPS = 1e-5
LN_EPS = 1e-5
LIMIT = 7.0
ALPHA = 1.702
RING = 8
PARTS = 4
SLOT = 2048


def hybrid_moe_step(nc, x_prompt, x_sample, state_pool, state_conv, g_mix, w_in, pool_w, pool_scale,
                    conv_w, conv_b, conv_ln_g, conv_ln_b, w_out, g_moe, w_router, b_router,
                    w_gate_up, b_gate_up, w_down, b_down, g_final,
                    y_prompt, y_sample, pool_prompt, conv_prompt, pool_sample, conv_sample,
                    normed_dram, rows_dram):
    _, SEQ, D = x_prompt.shape
    NB, NT, _ = x_sample.shape
    NS = NB * NT
    T = SEQ + NS
    CH = pool_scale.shape[1]
    G = CH // P
    TAPS = conv_w.shape[1]
    PB, CB = state_pool.shape[2], state_conv.shape[2]
    E = w_router.shape[2]
    K = D // P
    FF = w_down.shape[2]
    KF = FF // P
    rows = [P] * (SEQ // P) + [NS]
    J = len(rows)
    MAX_OVER = TOP_K * T // P
    COLS = E + MAX_OVER + 2
    GU_CHUNKS, DN_CHUNKS = K, KF // 2
    IN_CHUNKS = ("glu", 0), ("pool", 0), ("pool", 1), ("glu", 1), ("glu", 2), ("glu", 3)
    assert LN_EPS == RMS_EPS
    assert D == 1024 and CH == 512 and FF == D and SEQ == 512 and NS == 64
    HALF = K // 2
    HT = T // 2
    NEGATIVE = 2
    AHEAD = 3
    PE_TAPS = 9
    EARLY = 2

    with ExitStack() as ctx:
        def sb(name, shape, dt=F32):
            return ctx.enter_context(nc.sbuf_tensor(name, shape, dt))

        def sem(name):
            return ctx.enter_context(nc.semaphore(name))

        ring = sb("ring", [P, PARTS, SLOT])
        h = sb("h", [P, J, D])
        row_bufs = sb("row_bufs", [P, 2, D])
        row_buf = [row_bufs[:, i, :] for i in range(2)]
        ident = sb("ident", [P, P])
        iota_s = sb("iota_s", [P, P])
        part = sb("part", [2 * E, 1])
        low = sb("low", [2 * E, 1])
        eps = sb("eps", [P, 1])
        ss = sb("ss", [P, 4, J])
        gates = sb("gates", [P, J, TOP_K])
        gsum = sb("gsum", [P, 2, J])
        passed = sb("passed", [P, E])
        score4 = sb("score4", [P, J, TOP_K])
        off = sb("off", [P, COLS])
        blk_i = sb("blk_i", [1, COLS], I32)
        cmp_sum = sb("cmp_sum", [P, COLS - E])
        selm = sb("selm", [2 * E, COLS])
        slot_tok = sb("slot_tok", [P, COLS], U32)
        slot_row = sb("slot_row", [P, COLS], U32)
        idx_cur = [sb(f"idx_cur{i}", [P, 1], U32) for i in range(2)]
        row_cur = [sb(f"row_cur{i}", [P, 1], U32) for i in range(2)]
        sel_cur = [sb(f"sel_cur{i}", [2 * E, P], F32R) for i in range(2)]
        nit_i = sb("nit_i", [P, 2], I32)
        ps = ctx.enter_context(nc.psum_tensor("ps", [P, 8, 512], F32))
        psg = ps[:, 4:6, :].rearrange("p b n -> p (b n)")
        psu = ps[:, 6:8, :].rearrange("p b n -> p (b n)")
        psd = ps[:, 2:4, :].rearrange("p b n -> p (b n)")
        pst = ps[:, 0:2, :].rearrange("p b n -> p (b n)")

        with ExitStack() as mix:
            def mb(name, shape, dt=F32):
                return mix.enter_context(nc.sbuf_tensor(name, shape, dt))

            wout = mb("wout", [P, K, D])
            shared = mb("shared", [P, 2, G * T])
            u_p = mb("u_p", [P, G, PB + SEQ])
            u_s = mb("u_s", [P, G, NB, PB + NT])
            glu_p = mb("glu_p", [P, G, CB + SEQ])
            glu_s = mb("glu_s", [P, G, NB, CB + NT])
            win_p = [mb(f"win_p{i}", [P, PB + SEQ]) for i in range(2)]
            win_s = [mb(f"win_s{i}", [P, NB, PB + NT]) for i in range(2)]
            centred = [mb(f"centred{i}", [P, CH]) for i in range(J)]
            stage = [mb(f"stage{i}", [P, D]) for i in range(2)]
            xT = [mb(f"xT{i}", [P, K, P]) for i in range(2)]
            sum_s = mb("sum_s", [P, NS])
            vec_rows = mb("vec_rows", [32, P])
            poolw = mb("poolw", [P, G, P])
            gmoe = mb("gmoe", [P, D])
            mixT = mb("mixT", [P, K, T])
            router = mb("router", [P, K, E])
            br = mb("br", [P, E])
            vecT = mb("vecT", [P, 32])
            cwT = mb("cwT", [P, G, TAPS])
            tap_diag = mb("tap_diag", [P, PE_TAPS, P])
            before = mb("before", [P, P], F16)
            ones = mb("ones", [P, P], F16)
            base1 = mb("base1", [P, E])
            inv = mb("inv", [P, PB])
            fix = mb("fix", [P, PB])
            mv = mb("mv", [P, J, 2])
            st = mb("st", [P, 6])
            lnr = mb("lnr", [P, 2, J])
            L = mb("L", [P, J, E])
            v8 = mb("v8", [P, J, 8])
            i8 = mb("i8", [P, J, 8], U32)
            idxf = mb("idxf", [P, J, TOP_K])
            mask = mb("mask", [P, J, E], F16)
            over4 = mb("over4", [E, J - 1])
            over = mb("over", [E, 1])
            over_before = mb("over_before", [E, E + 1], F16)
            shift = mb("shift", [P, E])
            moved = mb("moved", [P, J, E])
            dest = mb("dest", [P, J, E])
            desti = mb("desti", [P, 3, J, TOP_K], I32)
            dmod = mb("dmod", [P, 2, J, TOP_K])
            limits = mb("limits", [E, J - 1])
            further = mb("further", [P, E])
            number = mb("number", [P, J, TOP_K])
        xnT = mixT
        yT = mixT
        conv = shared[:, 0, :].rearrange("p (c t) -> p c t", c=G)
        z = shared[:, 1, :].rearrange("p (c t) -> p c t", c=G)
        junk = [xT[i][:].rearrange("p k t -> p (k t)") for i in range(2)]
        cw_rows = stage[0][0:TAPS, CH:2 * CH]
        sp_rows = stage[0][0:NB * PB, 0:CH]
        sc_rows = stage[1][0:NB // 2 * CB, :].rearrange("p (a n) -> p a n", a=2)
        tails = [stage[0][:, 512:1024], stage[1][:, 0:512]]
        newest = [xT[i][:, 0:2, :].rearrange("p k t -> p (k t)").rearrange("p (c t) -> p c t", c=G) for i in range(2)]
        u_flat, z_flat = u_p[:].rearrange("p c t -> p (c t)"), shared[:, 1, :]
        pool_out = [u_flat[:, 0:D], u_flat[:, D:2 * D], z_flat[:, 0:D], z_flat[:, D:2 * D],
                    xT[0][:].rearrange("p k t -> p (k t)")]
        diag = row_buf[0][:, 0:J * P].rearrange("p (j t) -> p j t", j=J)
        taps_s = row_bufs[:].rearrange("p a n -> p (a n)")[:, 0:NS * TAPS].rearrange("p (b t k) -> p b t k", b=NB, k=TAPS)
        spare = mixT[:, :, :].rearrange("p k t -> p (k t)")
        oh = spare[:, 2048:2048 + J * TOP_K * E].rearrange("p (j k e) -> p j k e", j=J, k=TOP_K)
        inA = spare[:, 2688:2688 + J * TOP_K * P // 2].bitcast(F16).rearrange("p (j k s) -> p j k s", j=J, k=TOP_K)
        inB = spare[:, 3968:3968 + J * TOP_K * COLS // 2].bitcast(F16).rearrange("p (j k n) -> p j k n", j=J, k=TOP_K)
        cmp = spare[:, 2048:2048 + (COLS - E) * E].rearrange("p (n e) -> p n e", e=E)
        raw_gu = glu_p[:].rearrange("p c t -> p (c t)")[0:2 * E, 0:2 * FF]
        raw_dn = glu_s[:].rearrange("p c b t -> p (c b t)")[0:2 * E, 0:D]

        ring_more = sb("ring_more", [P, RING - PARTS, SLOT])
        bias = sb("bias", [2 * E, 2 * FF + D], F32R)
        w_hi = sb("w_hi", [P, PARTS, SLOT], F32R)
        w_lo = sb("w_lo", [P, PARTS, SLOT], F32R)
        x_lo = sb("x_lo", [P, K, P], F32R)
        h_hi, h_lo = sb("h_hi", [P, KF, P], F32R), sb("h_lo", [P, KF, P], F32R)
        y_sb = [sb(f"y_sb{i}", [P, D]) for i in range(2)]
        x_hi = sb("x_hi", [P, K, P], F32R)
        gate_s, up_s = sb("gate_s", [P, FF]), sb("up_s", [P, FF])
        gfin = up_s

        gmixT = vecT[:, 0:8]
        pscale, convb, lng, lnb = (vecT[:, 16 + 4 * n:20 + 4 * n] for n in range(4))

        s_cst = sem("s_cst")
        s_pad = sem("s_pad")
        s_vec = sem("s_vec")
        s_state = sem("s_state")
        s_x = [sem(f"s_x{j}") for j in range(J)]
        s_ring = [sem(f"s_ring{n}") for n in range(RING)]
        s_win = sem("s_win")
        s_hi, s_lo = sem("s_hi"), sem("s_lo")
        s_used = sem("s_used")
        s_wout, s_gmoe, s_biasp, s_dsel = sem("s_wout"), sem("s_gmoe"), sem("s_biasp"), sem("s_dsel")
        s_x_hi, s_x_lo, s_h_hi, s_h_lo = (sem(n) for n in ("s_x_hi", "s_x_lo", "s_h_hi", "s_h_lo"))
        s_poolw, s_router, s_bias, s_gfin = sem("s_poolw"), sem("s_router"), sem("s_bias"), sem("s_gfin")
        s_tsmall, s_small = sem("s_tsmall"), sem("s_small")
        s_ss, s_xr, s_tx, s_xnT = (sem(n) for n in ("s_ss", "s_xr", "s_tx", "s_xnT"))
        s_proj, s_val, s_glu, s_u, s_convp, s_convs, s_z, s_pm, s_pool = (
            sem(n) for n in ("s_proj", "s_val", "s_glu", "s_u", "s_convp", "s_convs", "s_z", "s_pm", "s_pool"))
        s_tail, s_tailev, s_cache, s_lnf, s_var, s_std, s_nrm, s_lnb, s_conv = (
            sem(n) for n in ("s_tail", "s_tailev", "s_cache", "s_lnf", "s_var", "s_std", "s_nrm", "s_lnb", "s_conv"))
        s_op, s_h, s_ss2, s_hr, s_rt, s_hnT, s_log, s_mask = (
            sem(n) for n in ("s_op", "s_h", "s_ss2", "s_hr", "s_rt", "s_hnT", "s_log", "s_mask"))
        s_vs, s_exp, s_rank, s_ab, s_inv, s_tab = (sem(n) for n in ("s_vs", "s_exp", "s_rank", "s_ab", "s_inv", "s_tab"))
        s_count, s_over, s_prefix = sem("s_count"), sem("s_over"), sem("s_prefix")
        s_idx, s_sel, s_txd, s_gu, s_gs, s_free, s_act, s_hdn = (
            sem(n) for n in ("s_idx", "s_sel", "s_txd", "s_gu", "s_gs", "s_free", "s_act", "s_hdn"))
        s_thd, s_down, s_y = (sem(n) for n in ("s_thd", "s_down", "s_y"))
        s_xg = [sem(f"s_xg{i}") for i in range(2)]
        s_yst = [sem(f"s_yst{i}") for i in range(2)]
        s_gat = [[sem(f"s_gat{a}_{i}") for i in range(J)] for a in range(2)]
        s_comb, s_ss3, s_fin, s_out = (sem(n) for n in ("s_comb", "s_ss3", "s_fin", "s_out"))
        s_L = sem("s_L")
        s_hrst = [sem(f"s_hrst{i}") for i in range(2)]
        s_tout = [sem(f"s_tout{i}") for i in range(2)]
        s_newest = sem("s_newest")
        s_half, s_halfev = sem("s_half"), sem("s_halfev")
        s_diag, s_taps = sem("s_diag"), sem("s_taps")
        s_row = sem("s_row")
        s_issued = sem("s_issued")
        s_chain = sem("s_chain")

        block = ctx.enter_context(nc.Block(no_gpsimd_drain=True))

        RING_BASE = [64, 64, 32, 32] + [0] * (RING - PARTS)
        PER_LOOP = 2 * (GU_CHUNKS + DN_CHUNKS)

        def gu_chunk(i0):
            return 0 if i0 == 0 else 12 * i0 - 4

        def dn_chunk(i0, last=False):
            return 12 * i0 + (8 if last else 16)

        def landed(c0, it):
            return RING_BASE[c0 % RING] + 16 * (c0 // RING + 1) + 16 * PER_LOOP // RING * it

        LAST = [J - 1, *range(J - 1)]

        def choices(n):
            j, s = LAST[n], 2 * n % PARTS
            return ring[0:rows[j], s:s + 2, :].rearrange("p s n -> p (s n)")

        def n_loops(eng):
            eng.wait_ge(s_tab, 2)
            return eng.value_load(nit_i[0:1, 1:2], min_val=E // 2 - 1, max_val=(E + MAX_OVER) // 2 - 1)

        def chunks_of(i0):
            return range(PARTS, GU_CHUNKS + AHEAD) if i0 == 0 else range(AHEAD if i0 == 1 else 0, GU_CHUNKS)

        def raw(c0):
            s = c0 % RING
            return ring[:, s, :] if s < PARTS else ring_more[:, s - PARTS, :]

        @block.sync
        def _(sp):
            for j in range(J):
                src = x_prompt[0, j * P:(j + 1) * P, :] if j < J - 1 else x_sample.rearrange("b t d -> (b t) d")
                sp.dma_start(h[0:rows[j], j, :], src).then_inc(s_x[j], 16)
            for v, r, a in ((g_mix, 0, 8), (g_moe, 8, 8), (pool_scale, 16, 4), (conv_b, 20, 4), (conv_ln_g, 24, 4), (conv_ln_b, 28, 4)):
                sp.dma_start(vec_rows[r:r + a, :], v[0].rearrange("(k p) -> k p", p=P)).then_inc(s_vec, 16)
            win = w_in[0].rearrange("(k p) n -> p k n", p=P)
            for q, (kind, n) in enumerate(IN_CHUNKS):
                if q >= PARTS:
                    sp.wait_ge(s_win, q - PARTS + 1)
                for a in range(2):
                    col = (2 * n + a) * P if kind == "pool" else CH + (a * G + n) * P
                    dst = ring[:, q % PARTS, a * K * P:(a + 1) * K * P].rearrange("p (k n) -> p k n", k=K)
                    sp.dma_start(dst, win[:, :, col:col + P]).then_inc(s_ring[q % PARTS], 16)
                if q == PARTS - 1:
                    sp.dma_start(poolw[:], pool_w[0].rearrange("g p n -> p g n")).then_inc(s_poolw, 16)
                    sp.dma_start(wout[:], w_out[0].rearrange("(k p) n -> p k n", p=P)).then_inc(s_wout, 16)

            sp.dma_start(router[:], w_router[0].rearrange("(k p) n -> p k n", p=P)).then_inc(s_router, 16)
            sp.dma_start(br[:], b_router.to_broadcast([P, E])).then_inc(s_router, 16)
            sp.dma_start(gmoe[:], g_moe.to_broadcast([P, D])).then_inc(s_gmoe, 16)
            sp.dma_start(pool_sample[0, :, 0:PB - NT, :], state_pool[0, :, NT:, :]).then_inc(s_cache, 16)
            sp.dma_start(conv_sample[0, :, 0:CB - NT, :], state_conv[0, :, NT:, :]).then_inc(s_cache, 16)

            def load(c0, it, src, a):
                if c0 >= RING:
                    sp.wait_ge(s_lo, c0 - RING + 1 + PER_LOOP * it)
                elif c0 < PARTS:
                    sp.wait_ge(s_win, (5, 6, 3, 4)[c0])
                else:
                    sp.wait_ge(s_op, J)
                dst = raw(c0).rearrange("p (a n) -> p a n", a=a) if a > 1 else raw(c0)
                sp.dma_start(dst, src).then_inc(s_ring[c0 % RING], 16)

            def load_gu(i0, it, e):
                w = w_gate_up[0, bass.ds(e, 1), :, :].rearrange("a (k p) n -> p (a k) n", p=P)
                for k in range(GU_CHUNKS):
                    load(gu_chunk(i0) + k, it, w[:, k, :], 1)

            def load_dn(i0, it, e, last=False):
                w = w_down[0, bass.ds(e, 1), :, :].rearrange("a (k p) n -> p (a k) n", p=P)
                for m in range(DN_CHUNKS):
                    load(dn_chunk(i0, last) + m, it, w[:, 2 * m:2 * m + 2, :], 2)

            load_gu(0, 0, 0)
            load_gu(1, 0, 1)
            load_dn(0, 0, 0)
            nit = n_loops(sp)
            with sp.Fori(0, nit) as it:
                e = [sp.value_load(blk_i[0:1, bass.ds(2 * it + n, 1)], min_val=0, max_val=E - 1) for n in (1, 2, 3)]
                for u in range(2):
                    load_gu(2 + u, it, e[u + 1])
                    load_dn(1 + u, it, e[u])
            e = sp.value_load(blk_i[0:1, bass.ds(2 * nit + 1, 1)], min_val=0, max_val=E - 1)
            load_dn(1, nit, e, last=True)
            sp.wait_ge(s_down, 2 + 2 * nit)
            sp.wait_ge(s_yst[0], 16 * (nit + 1))
            sp.wait_ge(s_yst[1], 16 * (nit + 1))
            for n, j in enumerate(LAST):
                if n >= PARTS // 2:
                    sp.wait_ge(s_comb, TOP_K * (n - PARTS // 2 + 1))
                src = rows_dram[j * P * TOP_K:(j * P + rows[j]) * TOP_K, :].rearrange("(p a k) n -> p a (k n)", a=2, k=TOP_K // 2)
                for a in range(2):
                    sp.dma_start(choices(n)[:, a * 2 * D:(a + 1) * 2 * D], src[:, a, :]).then_inc(s_gat[a][j], 16)

        @block.gpsimd
        def _(g):
            g.memset(ident[:], 0.0).then_inc(s_pad, 1)
            g.memset(before[:], 1.0).then_inc(s_pad, 1)
            g.memset(u_p[:, :, 0:PB], 0.0).then_inc(s_pad, 1)
            g.memset(glu_p[:, :, 0:CB], 0.0).then_inc(s_pad, 1)
            g.memset(ss[:], 1.0).then_inc(s_pad, 1)
            g.memset(mv[:], 1.0).then_inc(s_pad, 1)
            g.memset(L[:], 0.0).then_inc(s_pad, 1)
            g.memset(eps[:], RMS_EPS).then_inc(s_pad, 1)
            g.memset(ones[:], 1.0).then_inc(s_cst, 1)
            g.iota(iota_s[:], pattern=[[1, P]], base=0, channel_multiplier=0, allow_small_or_imprecise_dtypes=True).then_inc(s_cst, 1)
            g.iota(base1[:], pattern=[[P, E]], base=0, channel_multiplier=0, allow_small_or_imprecise_dtypes=True).then_inc(s_cst, 1)
            g.iota(part[:], pattern=[[0, 1]], base=0, channel_multiplier=1, allow_small_or_imprecise_dtypes=True).then_inc(s_cst, 1)
            for j0, j1, off in ((0, NEGATIVE, NEGATIVE * P * TOP_K), (NEGATIVE, J, NEGATIVE * P * TOP_K - 1)):
                g.iota(number[:, j0:j1, :], pattern=[[P * TOP_K, j1 - j0], [1, TOP_K]], base=j0 * P * TOP_K - off,
                       channel_multiplier=TOP_K, allow_small_or_imprecise_dtypes=True).then_inc(s_cst, 1)
            g.iota(limits[:], pattern=[[P, J - 1]], base=P, channel_multiplier=0, allow_small_or_imprecise_dtypes=True).then_inc(s_cst, 1)
            g.iota(further[:], pattern=[[-P, E]], base=P * (E - 1), channel_multiplier=0, allow_small_or_imprecise_dtypes=True).then_inc(s_cst, 1)
            g.iota(inv[:], pattern=[[1, PB]], base=1, channel_multiplier=0, allow_small_or_imprecise_dtypes=True).then_inc(s_cst, 1)
            g.wait_ge(s_pad, 8)
            g.affine_select(out=ident[:], in_=ident[:], compare_op=ALU.not_equal, fill=1.0, base=0,
                            pattern=[[-1, P]], channel_multiplier=1).then_inc(s_cst, 1)
            g.affine_select(out=before[:], in_=before[:], compare_op=ALU.is_gt, fill=0.0, base=0,
                            pattern=[[1, P]], channel_multiplier=-1).then_inc(s_cst, 1)

            g.dma_start(cw_rows, conv_w[0]).then_inc(s_state, 16)
            g.dma_start(sp_rows, state_pool[0].rearrange("b r c -> (b r) c")).then_inc(s_state, 16)
            for a in range(2):
                g.dma_start(sc_rows[:, a, :], state_conv[0, a * NB // 2:(a + 1) * NB // 2].rearrange("b r c -> (b r) c")).then_inc(s_state, 16)

            def gather(n0, it):
                n = n0 + 2 * it
                b = n0 % 2
                g.wait_ge(s_idx, n + 1)
                if n0 >= 2:
                    g.wait_ge(s_txd, n - 1)
                g.sem_inc(s_issued, 1)
                g.indirect_dma_start(row_buf[b][:, :], None, normed_dram[:, :],
                                     bass.IndirectOffsetOnAxis(ap=idx_cur[b][:, 0:1], axis=0),
                                     bounds_check=T - 1, oob_is_err=False).then_inc(s_xg[b], 16)

            def scatter(i0, it):
                i, b = i0 + 2 * it, i0 % 2
                g.wait_ge(s_row, i + 1)
                g.wait_ge(s_y, i + 1)
                g.sem_inc(s_issued, 1)
                g.indirect_dma_start(rows_dram[:, :], bass.IndirectOffsetOnAxis(ap=row_cur[b][:, 0:1], axis=0),
                                     y_sb[b][:, :], None, bounds_check=TOP_K * T - 1, oob_is_err=False).then_inc(s_yst[b], 16)

            for n, (src, own, ready) in enumerate(((u_s, PB, s_u), (glu_s, CB, s_glu))):
                g.wait_ge(ready, G)
                g.tensor_copy(newest[n].rearrange("p c (b t) -> p c b t", b=NB), src[:, :, :, own:]).then_inc(s_newest, 1)
            g.wait_ge(s_hrst[0], 16 * 3)
            g.wait_ge(s_hrst[1], 16 * 2)
            for n0 in range(4):
                gather(n0, 0)
            nit = n_loops(g)
            with g.Fori(0, nit) as it:
                for u in range(2):
                    scatter(u, it)
                    gather(4 + u, it)
            scatter(0, nit)
            scatter(1, nit)

        @block.scalar
        def _(act):
            act.wait_ge(s_pad, 8)
            for j in range(J):
                act.wait_ge(s_x[j], 16)
                act.activation(out=junk[j % 2][0:rows[j], :], in_=h[0:rows[j], j, :], func=ACT.Square,
                               accum_out=ss[0:rows[j], 0, j:j + 1]).then_inc(s_ss, 1)
                act.wait_ge(s_ss, j + 1)
            act.activation(out=ss[:, 1, :], in_=ss[:, 0, :], func=ACT.Sqrt, scale=1.0 / D, bias=eps[:]).then_inc(s_ss, 1)
            act.wait_ge(s_small, 5)
            for n in range(PE_TAPS):
                t = TAPS - PE_TAPS + n
                last = act.activation(out=tap_diag[:, n, :], in_=ident[:], func=ACT.Copy, scale=cwT[:, G - 1, t:t + 1])
            last.then_inc(s_diag, 1)
            for q, (kind, n) in enumerate(IN_CHUNKS):
                act.wait_ge(s_proj, q + 1)
                b = 4 * (q % 2)

                def evacuate(b, dst_p, dst_s):
                    act.activation(out=dst_p[:, 0:HT], in_=ps[:, b, 0:HT], func=ACT.Copy)
                    act.activation(out=dst_p[:, HT:SEQ], in_=ps[:, b + 1, 0:SEQ - HT], func=ACT.Copy)
                    return act.activation(out=dst_s, in_=ps[:, b + 1, SEQ - HT:HT].rearrange("p (b t) -> p b t", b=NB), func=ACT.Copy)

                if kind == "pool":
                    for a in range(2):
                        g_ = 2 * n + a
                        last = evacuate(b + 2 * a, u_p[:, g_, PB:], u_s[:, g_, :, PB:])
                        last.then_inc(s_u, 1)
                else:
                    act.activation(out=conv[:, n, :].rearrange("p (a t) -> p a t", a=2), in_=ps[:, b + 2:b + 4, 0:HT], func=ACT.Sigmoid)
                    evacuate(b, glu_p[:, n, CB:], glu_s[:, n, :, CB:]).then_inc(s_val, 1)

            def tail(n, bank, r, dma):
                act.wait_ge(s_tail, n + 1)
                if n >= 2:
                    act.wait_ge(s_tout[n % 2], 16)
                act.activation(out=tails[n % 2][0:r, :], in_=ps[0:r, bank, :], func=ACT.Copy).then_inc(s_tailev, 1)
                act.wait_ge(s_tailev, n + 1)
                act.dma_start(dma, tails[n % 2][0:r, :]).then_inc(s_tout[n % 2], 16)
            act.wait_ge(s_tsmall, 1)
            tail(0, 4, PB, pool_prompt[0, 0])
            tail(1, 5, NS, pool_sample[0, :, PB - NT:, :])
            for g_ in range(G):
                act.wait_ge(s_pm, g_ + 1)
                act.activation(out=yT[:, g_, 0:SEQ], in_=ps[:, g_, :], func=ACT.Copy, scale=pscale[:, g_:g_ + 1]).then_inc(s_pool, 1)
            act.wait_ge(s_pm, G + 1)
            for g_ in range(G):
                act.activation(out=yT[:, g_, SEQ:T], in_=ps[:, 6, g_ * NS:(g_ + 1) * NS], func=ACT.Copy,
                               scale=pscale[:, g_:g_ + 1]).then_inc(s_pool, 1)
            for j in range(J):
                if j == J - 1:
                    act.wait_ge(s_var, J)
                    act.activation(out=lnr[:, 0, :], in_=mv[:, :, 1], func=ACT.Sqrt, bias=eps[:]).then_inc(s_std, 1)
                b = 6 - 2 * (j % 2)
                act.wait_ge(s_half, j + 1)
                act.activation(out=pool_out[j][0:rows[j], :], in_=ps[0:rows[j], b:b + 2, :].rearrange("p b n -> p (b n)"),
                               func=ACT.Copy).then_inc(s_halfev, 1)
                if j == J - 3:
                    tail(2, 0, CB, conv_prompt[0, 0])
                    tail(3, 1, NS, conv_sample[0, :, CB - NT:, :])
            for j in range(J):
                act.wait_ge(s_lnb, j + 1)
                for c in range(G):
                    act.activation(out=yT[:, G + c, j * P:j * P + rows[j]], in_=ps[:, j, c * P:c * P + rows[j]],
                                   func=ACT.Silu, scale=lng[:, c:c + 1], bias=lnb[:, c:c + 1]).then_inc(s_conv, 1)
            def high(c0, it):
                act.wait_ge(s_ring[c0 % RING], landed(c0, it))
                if c0 >= PARTS:
                    act.wait_ge(s_used, c0 - PARTS + 1 + PER_LOOP * it)
                act.activation(out=w_hi[:, c0 % PARTS, :], in_=raw(c0), func=ACT.Copy).then_inc(s_hi, 1)

            for n in range(2):
                act.wait_ge(s_tout[n], 32)
            for a in range(2):
                act.dma_start(raw_gu[a * E:(a + 1) * E, :], b_gate_up[0]).then_inc(s_bias, 16)
                act.dma_start(raw_dn[a * E:(a + 1) * E, :], b_down[0]).then_inc(s_bias, 16)
            for j in range(J):
                r = rows[j]
                act.wait_ge(s_h, J + j + 1)
                act.activation(out=junk[j % 2][0:r, :], in_=h[0:r, j, :], func=ACT.Square,
                               accum_out=ss[0:r, 0, j:j + 1]).then_inc(s_ss2, 1)
                act.wait_ge(s_ss2, 2 * j + 1)
                act.activation(out=ss[0:r, 1, j:j + 1], in_=ss[0:r, 0, j:j + 1], func=ACT.Sqrt, scale=1.0 / D,
                               bias=eps[0:r, :]).then_inc(s_ss2, 1)
                act.wait_ge(s_hr, j + 1)
                act.dma_start(normed_dram[j * P:j * P + r, :], row_buf[j % 2][0:r, :]).then_inc(s_hrst[j % 2], 16)
                for half in range(2):
                    act.wait_ge(s_rt, 2 * j + half + 1)
                    act.activation(out=xT[j % 2][:, HALF * half:HALF * half + HALF, 0:r],
                                   in_=ps[:, half, :].rearrange("p (k t) -> p k t", k=HALF)[:, :, 0:r],
                                   func=ACT.Copy).then_inc(s_hnT, 1)
                if j == 0:
                    act.wait_ge(s_bias, 64)
                    act.activation(out=bias[:, 0:2 * FF], in_=raw_gu, func=ACT.Copy).then_inc(s_biasp, 1)
                    act.activation(out=bias[:, 2 * FF:], in_=raw_dn, func=ACT.Copy).then_inc(s_biasp, 1)
                elif j <= EARLY:
                    high(j - 1, 0)
            act.wait_ge(s_biasp, 3)
            for c in range(EARLY, PARTS):
                high(c, 0)
            act.wait_ge(s_vs, 1)
            act.activation(out=gates[:], in_=score4[:], func=ACT.Exp).then_inc(s_exp, 1)

            def x_high(i0, it):
                act.wait_ge(s_txd, i0 + 1 + 2 * it)
                act.activation(out=x_hi[:].rearrange("p k t -> p (k t)"), in_=pst, func=ACT.Copy).then_inc(s_x_hi, 1)

            def h_high(i0, it):
                act.wait_ge(s_thd, i0 + 1 + 2 * it)
                act.activation(out=h_hi[:].rearrange("p k t -> p (k t)"), in_=pst, func=ACT.Copy, scale=1.0 / ALPHA).then_inc(s_h_hi, 1)

            def silu(i0, it):
                act.wait_ge(s_gs, i0 + 1 + 2 * it)
                act.activation(out=gate_s[:], in_=gate_s[:], func=ACT.Silu, scale=ALPHA).then_inc(s_act, 1)

            def result(i0, it):
                act.wait_ge(s_row, i0 + 1 + 2 * it)
                act.wait_ge(s_down, i0 + 1 + 2 * it)
                act.activation(out=y_sb[i0 % 2][:], in_=psd, func=ACT.Copy).then_inc(s_y, 1)

            def step(i0, it):
                for k in chunks_of(i0):
                    high(gu_chunk(i0) + k, it)
                    if k == GU_CHUNKS // 2 - 1:
                        if i0 >= 2:
                            result(i0 - 2, it)
                        if i0 >= 1:
                            h_high(i0 - 1, it)
                if i0 >= 1:
                    for m in range(DN_CHUNKS):
                        high(dn_chunk(i0 - 1) + m, it)
                x_high(i0 + 1, it)
                silu(i0, it)

            x_high(0, 0)
            step(0, 0)
            act.wait_ge(s_tab, 1)
            step(1, 0)
            nit = n_loops(act)
            with act.Fori(0, nit) as it:
                step(2, it)
                step(3, it)
            result(0, nit)
            h_high(1, nit)
            for m in range(DN_CHUNKS):
                high(dn_chunk(1, last=True) + m, nit)
            result(1, nit)
            act.dma_start(gfin[:], g_final.rearrange("(a n) -> a n", a=1).to_broadcast([P, D])).then_inc(s_gfin, 16)

            def store(n):
                j = LAST[n]
                act.wait_ge(s_fin, n + 1)
                dst = y_prompt[0, j * P:(j + 1) * P, :] if j < J - 1 else y_sample.rearrange("b t d -> (b t) d")
                act.dma_start(dst, h[0:rows[j], j, :]).then_inc(s_out, 16)

            for n, j in enumerate(LAST):
                r = rows[j]
                act.wait_ge(s_comb, TOP_K * (n + 1))
                act.activation(out=gate_s[0:r, :], in_=h[0:r, j, :], func=ACT.Square,
                               accum_out=ss[0:r, 0, j:j + 1]).then_inc(s_ss3, 1)
                act.wait_ge(s_ss3, 2 * n + 1)
                act.activation(out=ss[0:r, 1, j:j + 1], in_=ss[0:r, 0, j:j + 1], func=ACT.Sqrt, scale=1.0 / D,
                               bias=eps[0:r, :]).then_inc(s_ss3, 1)
                if n:
                    store(n - 1)
            store(J - 1)
            act.wait_ge(s_out, 16 * J)
            act.wait_ge(s_cache, 32)

        @block.vector
        def _(dve):
            chain = [0]

            def link(ins):
                chain[0] += 1
                ins.then_inc(s_chain, 1)
                dve.wait_ge(s_chain, chain[0])

            dve.wait_ge(s_cst, 11)
            link(dve.reciprocal(inv[:], inv[:]))
            link(dve.tensor_scalar(low[:], part[:], float(E), float(-E), ALU.is_ge, ALU.mult))
            link(dve.tensor_tensor(low[:], low[:], part[:], ALU.add))
            dve.tensor_scalar(selm[:, 0:E], iota_s[0:2 * E, 0:E], low[:], None, ALU.is_equal)
            dve.tensor_copy(blk_i[:, 0:E], iota_s[0:1, 0:E])
            dve.wait_ge(s_tsmall, 1)
            dve.tensor_copy(vecT[:], ps[:, 6, 0:32]).then_inc(s_small, 1)
            dve.wait_ge(s_small, 1)
            dve.wait_ge(s_ss, J + 1)
            link(dve.reciprocal(ss[:, 2, :], ss[:, 1, :]))
            for j in range(J):
                dve.tensor_scalar(diag[:, j, :], ident[:], ss[:, 2, j:j + 1], None, ALU.mult).then_inc(s_xr, 1)

            for j in range(J):
                r = rows[j]
                for half in range(2):
                    ks = slice(HALF * half, HALF * half + HALF)
                    dve.wait_ge(s_tx, 2 * j + half + 1)
                    dve.tensor_tensor(xnT[:, ks, j * P:j * P + r],
                                      ps[:, 2 * (j % 2) + half, :].rearrange("p (k t) -> p k t", k=HALF)[:, :, 0:r],
                                      gmixT[:, ks].unsqueeze(2).to_broadcast([P, HALF, r]), ALU.mult).then_inc(s_xnT, 1)

            dve.wait_ge(s_tsmall, 2)
            dve.tensor_copy(cwT[:].rearrange("p c t -> p (c t)"), ps[:, 6, 32:32 + G * TAPS]).then_inc(s_small, 1)
            dve.tensor_copy(u_s[:, :, :, 0:PB], ps[:, 4, 0:G * NB * PB].rearrange("p (c b r) -> p c b r", c=G, b=NB)).then_inc(s_small, 1)
            for a in range(2):
                dve.tensor_copy(glu_s[:, :, a * NB // 2:(a + 1) * NB // 2, 0:CB],
                                ps[:, 5 + 2 * a, 0:G * NB // 2 * CB].rearrange("p (c b r) -> p c b r", c=G, b=NB // 2)).then_inc(s_small, 1)
            dve.wait_ge(s_small, 5)

            dve.wait_ge(s_pad, 8)
            odd_p = win_p[0][:, 0:SEQ]

            def convolve(q0, it, taps=TAPS):
                q = q0 + it
                acc_p = conv[:, bass.ds(q, 1), 0:SEQ].rearrange("p a t -> p (a t)")
                acc_s = conv[:, bass.ds(q, 1), SEQ:T].rearrange("p a t -> p (a t)")
                val_p = glu_p[:, bass.ds(q, 1), CB:].rearrange("p a t -> p (a t)")
                val_s = glu_s[:, bass.ds(q, 1), :, CB:].rearrange("p a b t -> p (a b) t")
                dve.wait_ge(s_val, q + 1)
                dve.tensor_tensor(val_p, val_p, acc_p, ALU.mult)
                dve.tensor_tensor(val_s, val_s, acc_s.rearrange("p (b t) -> p b t", b=NB), ALU.mult).then_inc(s_glu, 1)
                dve.wait_ge(s_glu, q + 1)
                cb = convb[:, bass.ds(q, 1)]
                for t in range(taps):
                    w = cwT[:, bass.ds(q, 1), t:t + 1].rearrange("p a t -> p (a t)")
                    src_p = glu_p[:, bass.ds(q, 1), t:t + SEQ].rearrange("p a t -> p (a t)")
                    if t == 0:
                        dve.tensor_scalar(acc_p, src_p, w, cb, ALU.mult, ALU.add).then_inc(s_convp, 1)
                    elif t == 1:
                        dve.tensor_scalar(odd_p, src_p, w, None, ALU.mult).then_inc(s_convp, 1)
                    else:
                        if t == NT + 1:
                            dve.wait_ge(s_convs, 3 * q + 1)
                        dve.wait_ge(s_convp, (TAPS + 1) * q + t - 1)
                        acc = odd_p if t % 2 else acc_p
                        dve.scalar_tensor_tensor(out=acc, in0=src_p, scalar=w, in1=acc, op0=ALU.mult, op1=ALU.add).then_inc(s_convp, 1)
                    if t < NT:
                        ws = cwT[:, bass.ds(q, 1), :].to_broadcast([P, NB, TAPS])
                        src_s = glu_s[:, bass.ds(q, 1), :, t:t + TAPS].rearrange("p a b k -> p (a b) k")
                        last = dve.tensor_tensor(taps_s[:, :, t, :], src_s, ws, ALU.mult)
                        if t == NT - 1:
                            last.then_inc(s_convs, 1)
                    elif t == NT + 1:
                        dve.tensor_reduce(sum_s[:], taps_s.rearrange("p b t k -> p (b t) k"), AX.X, ALU.add).then_inc(s_convs, 1)
                    elif t == NT + 3:
                        dve.wait_ge(s_convs, 3 * q + 2)
                        dve.tensor_scalar(acc_s, sum_s[:], cb, None, ALU.add).then_inc(s_convs, 1)
                dve.wait_ge(s_convp, (TAPS + 1) * q + taps)
                dve.tensor_tensor(acc_p, acc_p, odd_p, ALU.add).then_inc(s_convp, 1)
                if taps < TAPS:
                    dve.wait_ge(s_convp, (TAPS + 1) * q + taps + 1)
                    dve.wait_ge(s_taps, 1)
                    dve.tensor_tensor(acc_p, acc_p, ps[:, 2, :], ALU.add).then_inc(s_convp, 1)

            convolve(0, 0)
            dve.wait_ge(s_convp, TAPS + 1)

            for g_, w in enumerate(WINDOWS):
                dve.wait_ge(s_u, g_ + 1)
                src_p, src_s = u_p[:, g_, :], u_s[:, g_, :, :]
                for m in range(g_ + 1):
                    lo, sh = 2 ** (m + 1) - 1, 2 ** m
                    dve.tensor_tensor(win_s[m % 2][:, :, lo:], src_s[:, :, lo:], src_s[:, :, lo - sh:PB + NT - sh], ALU.add)
                    link(dve.tensor_tensor(win_p[m % 2][:, lo:], src_p[:, lo:], src_p[:, lo - sh:PB + SEQ - sh], ALU.add))
                    src_p, src_s = win_p[m % 2][:, :], win_s[m % 2][:, :, :]
                dve.scalar_tensor_tensor(out=z[:, g_, SEQ:T].rearrange("p (b t) -> p b t", b=NB), in0=src_s[:, :, PB:], scalar=1.0 / w,
                                         in1=u_s[:, g_, :, PB:], op0=ALU.mult, op1=ALU.subtract)
                dve.tensor_tensor(fix[:, 0:w - 1], src_p[:, PB:PB + w - 1], inv[:, 0:w - 1], ALU.mult)
                link(dve.scalar_tensor_tensor(out=z[:, g_, 0:SEQ], in0=src_p[:, PB:], scalar=1.0 / w, in1=u_p[:, g_, PB:],
                                              op0=ALU.mult, op1=ALU.subtract))
                dve.tensor_tensor(z[:, g_, 0:w - 1], fix[:, 0:w - 1], u_p[:, g_, PB:PB + w - 1], ALU.subtract).then_inc(s_z, 1)
                dve.wait_ge(s_z, g_ + 1)

            with dve.Fori(0, G - 2) as it:
                convolve(1, it)
            convolve(G - 1, 0, TAPS - PE_TAPS)

            for j in range(J):
                r, bank = rows[j], (0, 1, 2, 3, 4)[j]
                dve.wait_ge(s_lnf, j + 1)
                link(dve.bn_stats(st[0:r, :], ps[0:r, bank, :]))
                dve.bn_aggr(mv[0:r, j, :], st[0:r, :]).then_inc(s_var, 1)
                dve.wait_ge(s_var, j + 1)
            dve.wait_ge(s_std, 1)
            link(dve.reciprocal(lnr[:, 1, :], lnr[:, 0, :]))
            for j in range(J):
                r, bank = rows[j], (0, 1, 2, 3, 4)[j]
                dve.tensor_scalar(centred[j][0:r, 0:CH], ps[0:r, bank, :], mv[0:r, j, 0:1], lnr[0:r, 1, j:j + 1],
                                  ALU.subtract, ALU.mult).then_inc(s_nrm, 1)
            for j in range(J):
                r = rows[j]
                dve.wait_ge(s_halfev, j + 1)
                dve.tensor_tensor(h[0:r, j, :], h[0:r, j, :], pool_out[j][0:r, :], ALU.add).then_inc(s_h, 1)

            def low_part(c0, it):
                dve.wait_ge(s_hi, c0 + 1 + PER_LOOP * it)
                dve.tensor_tensor(w_lo[:, c0 % PARTS, :], raw(c0), w_hi[:, c0 % PARTS, :].bitcast(F32),
                                  ALU.subtract).then_inc(s_lo, 1)

            dve.wait_ge(s_gmoe, 16)
            def topk(j):
                r = rows[j]
                dve.wait_ge(s_log, j + 1)
                dve.tensor_tensor(L[0:r, j, :], ps[0:r, 4, j * E:(j + 1) * E], br[0:r, :], ALU.add).then_inc(s_L, 1)
                dve.wait_ge(s_L, j + 1)
                link(dve.max(v8[:, j, :], L[:, j, :]))
                link(dve.max_index(i8[:, j, :], v8[:, j, :], L[:, j, :]))
                link(dve.tensor_copy(idxf[:, j, :], i8[:, j, 0:TOP_K]))
                link(dve.tensor_tensor(oh[:, j], iota_s[:, 0:E].unsqueeze(1).to_broadcast([P, TOP_K, E]),
                                       idxf[:, j, :].unsqueeze(2).to_broadcast([P, TOP_K, E]), ALU.is_equal))
                with nc.allow_low_precision(reason="sums of at most one 1"):
                    dve.tensor_reduce(mask[:, j, :], oh[:, j].rearrange("p k e -> p e k"), AX.X, ALU.add).then_inc(s_mask, 1)

            dve.wait_ge(s_router, 32)
            for j in range(J):
                r, b = rows[j], 6 - 4 * (j % 2)
                dve.wait_ge(s_op, j + 1)
                dve.wait_ge(s_h, J + j)
                dve.tensor_tensor(h[0:r, j, :], h[0:r, j, :], ps[0:r, b:b + 2, :].rearrange("p b n -> p (b n)"), ALU.add).then_inc(s_h, 1)
                dve.wait_ge(s_ss2, 2 * j + 2)
                link(dve.reciprocal(ss[0:r, 3, j:j + 1], ss[0:r, 1, j:j + 1]))
                if j >= 2:
                    dve.wait_ge(s_rt, 2 * (j - 1))
                    dve.wait_ge(s_hrst[j % 2], 16 * (j // 2))
                dve.scalar_tensor_tensor(out=row_buf[j % 2][0:r, :], in0=h[0:r, j, :], scalar=ss[0:r, 3, j:j + 1],
                                         in1=gmoe[0:r, :], op0=ALU.mult, op1=ALU.mult).then_inc(s_hr, 1)
                if j >= 1:
                    topk(j - 1)
                if j == 1:
                    dve.wait_ge(s_biasp, 2)
                    dve.tensor_tensor(bias[E:2 * E, 0:2 * FF], raw_gu[E:2 * E, :], bias[E:2 * E, 0:2 * FF].bitcast(F32), ALU.subtract)
                    dve.tensor_tensor(bias[E:2 * E, 2 * FF:], raw_dn[E:2 * E, :], bias[E:2 * E, 2 * FF:].bitcast(F32),
                                      ALU.subtract).then_inc(s_biasp, 1)
                elif j >= 2 and j < 2 + EARLY:
                    low_part(j - 2, 0)
            topk(J - 1)

            dve.tensor_tensor(score4[:], v8[:, :, 0:TOP_K], v8[:, :, 0:1].to_broadcast([P, J, TOP_K]), ALU.subtract).then_inc(s_vs, 1)

            dve.wait_ge(s_count, 1)
            link(dve.tensor_tensor(over4[:], ps[0:E, 2, 0:J - 1], limits[:], ALU.is_gt))
            link(dve.tensor_reduce(over[:], over4[:], AX.X, ALU.add))
            dve.tensor_scalar(over_before[:], before[0:E, 0:E + 1], over[:], None, ALU.mult).then_inc(s_over, 1)
            dve.wait_ge(s_rank, 1)
            rank = ps[:, 5, 0:J * E].rearrange("p (j e) -> p j e", j=J)
            dve.tensor_tensor(dest[:], rank, base1[:].unsqueeze(1).to_broadcast([P, J, E]), ALU.add)
            dve.wait_ge(s_prefix, 1)
            link(dve.scalar_tensor_tensor(out=shift[:], in0=ps[:, 3, 0:E], scalar=float(P), in1=further[:], op0=ALU.mult, op1=ALU.add))
            link(dve.scalar_tensor_tensor(out=moved[:], in0=rank, scalar=float(P), in1=shift[:].unsqueeze(1).to_broadcast([P, J, E]),
                                          op0=ALU.is_ge, op1=ALU.mult))
            link(dve.tensor_tensor(dest[:], dest[:], moved[:], ALU.add))
            link(dve.tensor_tensor(oh, oh, dest[:].unsqueeze(2).to_broadcast([P, J, TOP_K, E]), ALU.mult))
            with nc.allow_low_precision(reason="whole numbers"):
                link(dve.tensor_reduce(desti[:, 0], oh, AX.X, ALU.add))
            dve.tensor_scalar(desti[:, 1], desti[:, 0], 7, None, ALU.arith_shift_right)
            link(dve.tensor_scalar(desti[:, 2], desti[:, 0], P - 1, None, ALU.bitwise_and))
            link(dve.tensor_copy(dmod[:], desti[:, 1:3]))
            link(dve.tensor_tensor(inB, iota_s[:, 0:COLS].unsqueeze(1).unsqueeze(1).to_broadcast([P, J, TOP_K, COLS]),
                                   dmod[:, 0].unsqueeze(3).to_broadcast([P, J, TOP_K, COLS]), ALU.is_equal))
            link(dve.tensor_tensor(inB, inB, number[:].unsqueeze(3).to_broadcast([P, J, TOP_K, COLS]), ALU.mult))
            for j in range(J):
                dve.tensor_tensor(inA[:, j], iota_s[:].unsqueeze(1).to_broadcast([P, TOP_K, P]),
                                  dmod[:, 1, j, :].unsqueeze(2).to_broadcast([P, TOP_K, P]), ALU.is_equal).then_inc(s_ab, 1)
            dve.tensor_copy(passed[:], ps[:, 3, 1:E + 1])
            dve.wait_ge(s_inv, 1)
            num = ps[:, 4, J * E:J * E + COLS]
            link(dve.tensor_scalar(off[:], num, 0.0, float(1 << 16), ALU.is_equal, ALU.mult))
            link(dve.scalar_tensor_tensor(out=off[:], in0=num, scalar=0.0, in1=off[:], op0=ALU.is_lt, op1=ALU.add))
            link(dve.scalar_tensor_tensor(out=slot_row[:], in0=num, scalar=float(NEGATIVE * P * TOP_K - 1), in1=off[:],
                                          op0=ALU.add, op1=ALU.add))
            link(dve.tensor_scalar(slot_tok[:], slot_row[:], 2, None, ALU.logical_shift_right))

            def tables():
                link(dve.tensor_tensor(cmp[:], iota_s[:, 0:COLS - E].unsqueeze(2).to_broadcast([P, COLS - E, E]),
                                       passed[:].unsqueeze(1).to_broadcast([P, COLS - E, E]), ALU.is_ge))
                link(dve.tensor_reduce(cmp_sum[:], cmp[:], AX.X, ALU.add))
                link(dve.tensor_scalar(cmp_sum[:], cmp_sum[:], float(E - 1), None, ALU.min))
                dve.tensor_scalar(selm[:, E:], cmp_sum[0:2 * E, :], low[:], None, ALU.is_equal)
                dve.tensor_copy(blk_i[:, E:], cmp_sum[0:1, :]).then_inc(s_tab, 1)
                link(dve.tensor_scalar(nit_i[:, 0:1], passed[:, E - 1:E], float(E - 1), None, ALU.add))
                dve.tensor_scalar(nit_i[:, 1:2], nit_i[:, 0:1], 1, None, ALU.arith_shift_right).then_inc(s_tab, 1)
                dve.wait_ge(s_exp, 1)
                link(dve.tensor_reduce(gsum[:, 0, :], gates[:], AX.X, ALU.add))
                link(dve.reciprocal(gsum[:, 1, :], gsum[:, 0, :]))
                link(dve.tensor_tensor(gates[:], gates[:], gsum[:, 1, :].unsqueeze(2).to_broadcast([P, J, TOP_K]), ALU.mult))

            def tokens(i0, it):
                b = i0 % 2
                if i0 >= 2:
                    dve.wait_ge(s_xg[b], 16 * (i0 // 2) + 16 * it)
                dve.tensor_copy(idx_cur[b][:], slot_tok[:, bass.ds(i0 + 2 * it, 1)]).then_inc(s_idx, 1)

            def places(i0, it):
                b = i0 % 2
                if i0 >= 2:
                    dve.wait_ge(s_yst[b], 16 * (i0 // 2) + 16 * it)
                dve.tensor_copy(row_cur[b][:], slot_row[:, bass.ds(i0 + 2 * it, 1)]).then_inc(s_row, 1)

            def select(i0, it):
                if i0 >= 2:
                    dve.wait_ge(s_dsel, i0 - 1 + 2 * it)
                dve.tensor_copy(sel_cur[i0 % 2][:], selm[:, bass.ds(i0 + 2 * it, 1)].to_broadcast([2 * E, P])).then_inc(s_sel, 1)

            def x_low(i0, it):
                dve.wait_ge(s_x_hi, i0 + 1 + 2 * it)
                dve.tensor_tensor(x_lo[:].rearrange("p k t -> p (k t)"), pst, x_hi[:].bitcast(F32).rearrange("p k t -> p (k t)"),
                                  ALU.subtract).then_inc(s_x_lo, 1)

            def h_low(i0, it):
                dve.wait_ge(s_h_hi, i0 + 1 + 2 * it)
                dve.scalar_tensor_tensor(out=h_lo[:].rearrange("p k t -> p (k t)"), in0=pst, scalar=1.0 / ALPHA,
                                         in1=h_hi[:].bitcast(F32).rearrange("p k t -> p (k t)"),
                                         op0=ALU.mult, op1=ALU.subtract).then_inc(s_h_lo, 1)

            def swiglu(i0, it):
                i = i0 + 2 * it
                dve.wait_ge(s_gu, i + 1)
                dve.tensor_scalar(gate_s[:], psg, LIMIT, None, ALU.min).then_inc(s_gs, 1)
                dve.tensor_scalar(up_s[:], psu, LIMIT, -LIMIT, ALU.min, ALU.max).then_inc(s_free, 1)
                dve.wait_ge(s_free, i + 1)
                dve.wait_ge(s_act, i + 1)
                dve.scalar_tensor_tensor(out=up_s[:], in0=up_s[:], scalar=1.0, in1=gate_s[:], op0=ALU.add, op1=ALU.mult).then_inc(s_hdn, 1)

            def step(i0, it):
                tokens(i0 + 2, it)
                for k in chunks_of(i0):
                    low_part(gu_chunk(i0) + k, it)
                    if k == GU_CHUNKS // 2 - 1 and i0 >= 1:
                        h_low(i0 - 1, it)
                if i0 >= 1:
                    for m in range(DN_CHUNKS):
                        low_part(dn_chunk(i0 - 1) + m, it)
                swiglu(i0, it)
                x_low(i0 + 1, it)
                select(i0 + 1, it)
                places(i0, it)

            tokens(0, 0)
            tokens(1, 0)
            select(0, 0)
            for c in range(EARLY, PARTS):
                low_part(c, 0)
            x_low(0, 0)
            tables()
            step(0, 0)
            step(1, 0)
            nit = n_loops(dve)
            with dve.Fori(0, nit) as it:
                step(2, it)
                step(3, it)
            h_low(1, nit)
            for m in range(DN_CHUNKS):
                low_part(dn_chunk(1, last=True) + m, nit)

            dve.wait_ge(s_gfin, 16)

            def normed(n):
                j = LAST[n]
                r = rows[j]
                dve.wait_ge(s_ss3, 2 * n + 2)
                link(dve.reciprocal(ss[0:r, 2, j:j + 1], ss[0:r, 1, j:j + 1]))
                dve.scalar_tensor_tensor(out=h[0:r, j, :], in0=h[0:r, j, :], scalar=ss[0:r, 2, j:j + 1], in1=gfin[0:r, :],
                                         op0=ALU.mult, op1=ALU.mult).then_inc(s_fin, 1)

            for n, j in enumerate(LAST):
                r = rows[j]
                for k in range(TOP_K):
                    if k % 2 == 0:
                        dve.wait_ge(s_gat[k // 2][j], 16)
                    if k:
                        dve.wait_ge(s_comb, n * TOP_K + k)
                    dve.scalar_tensor_tensor(out=h[0:r, j, :], in0=choices(n)[:, k * D:(k + 1) * D], scalar=gates[0:r, j, k:k + 1],
                                             in1=h[0:r, j, :], op0=ALU.mult, op1=ALU.add).then_inc(s_comb, 1)
                if n:
                    normed(n - 1)
            normed(J - 1)

        @block.tensor
        def _(pe):
            pe.wait_ge(s_cst, 11)
            pe.wait_ge(s_vec, 16 * 6)
            pe.transpose(ps[:, 6, 0:32], vec_rows[:], ident[0:32, 0:32]).then_inc(s_tsmall, 1)

            def turn(src, r, first, ready, done):
                for half in range(2):
                    if first is not None:
                        pe.wait_ge(ready, first + half)
                    for m in range(HALF):
                        k = HALF * half + m
                        last = pe.transpose(ps[:, half, m * P:m * P + r], src[0:r, k * P:(k + 1) * P], ident[0:r, 0:r])
                    last.then_inc(done, 1)

            for j in range(J):
                r = rows[j]
                pe.wait_ge(s_xr, j + 1)
                for half in range(2):
                    if j >= 2:
                        pe.wait_ge(s_xnT, 2 * j - 3 + half)
                    for m in range(HALF):
                        k = HALF * half + m
                        last = pe.matmul(ps[:, 2 * (j % 2) + half, m * P:m * P + r], lhsT=h[0:r, j, k * P:(k + 1) * P], rhs=diag[0:r, j, 0:r],
                                         start=True, stop=True)
                    last.then_inc(s_tx, 1)

            pe.wait_ge(s_state, 16 * 4)
            pe.wait_ge(s_small, 1)
            for c in range(G):
                pe.transpose(ps[:, 6, 32 + c * TAPS:32 + (c + 1) * TAPS], cw_rows[:, c * P:(c + 1) * P], ident[0:TAPS, 0:TAPS])
                n = NB * PB
                pe.transpose(ps[:, 4, c * n:(c + 1) * n], sp_rows[:, c * P:(c + 1) * P], ident[0:n, 0:n])
                n = NB // 2 * CB
                for a in range(2):
                    last = pe.transpose(ps[:, 5 + 2 * a, c * n:(c + 1) * n], sc_rows[:, a, c * P:(c + 1) * P], ident[0:n, 0:n])
            last.then_inc(s_tsmall, 1)
            pe.wait_ge(s_xnT, 2 * J)

            for q in range(len(IN_CHUNKS)):
                pe.wait_ge(s_ring[q % PARTS], 32 * (q // PARTS + 1))
                b = 4 * (q % 2)
                if q == 1:
                    pe.wait_ge(s_small, 5)
                if q in (2, 4, 5):
                    pe.wait_ge(s_val, q // 2)
                elif q == 3:
                    pe.wait_ge(s_u, 2)
                if q == 4:
                    pe.wait_ge(s_u, 4)
                for a in range(2):
                    w = ring[:, q % PARTS, a * K * P:(a + 1) * K * P].rearrange("p (k n) -> p k n", k=K)
                    for k in range(K):
                        for n in range(2):
                            last = pe.matmul(ps[:, b + 2 * a + n, 0:HT], lhsT=w[:, k, :], rhs=xnT[:, k, n * HT:(n + 1) * HT],
                                             start=k == 0, stop=k == K - 1)
                last.then_inc(s_proj, 1)
                pe.wait_ge(s_proj, q + 1)
                pe.sem_inc(s_win, 1)

            pe.wait_ge(s_val, G)
            def tails_of(src, r, bank):
                for c in range(G):
                    last = pe.transpose(ps[0:r, bank, c * P:(c + 1) * P], src(c), ident[:])
                last.then_inc(s_tail, 1)
            tails_of(lambda c: u_p[:, c, PB + SEQ - PB:], PB, 4)
            pe.wait_ge(s_newest, 1)
            tails_of(lambda c: newest[0][:, c, :], NS, 5)
            pe.wait_ge(s_poolw, 16)
            pe.wait_ge(s_z, G)
            for g_ in range(G):
                pe.matmul(ps[:, g_, :], lhsT=poolw[:, g_, :], rhs=z[:, g_, 0:SEQ], start=True, stop=True).then_inc(s_pm, 1)
            for g_ in range(G):
                last = pe.matmul(ps[:, 6, g_ * NS:(g_ + 1) * NS], lhsT=poolw[:, g_, :], rhs=z[:, g_, SEQ:T],
                                 start=True, stop=True)
            last.then_inc(s_pm, 1)

            def output(j, b, k0, done):
                r = rows[j]
                for k in range(k0, k0 + G):
                    for n in range(2):
                        last = pe.matmul(ps[0:r, b + n, :], lhsT=yT[:, k, j * P:j * P + r], rhs=wout[:, k, n * 512:(n + 1) * 512],
                                         start=k == k0, stop=k == k0 + G - 1)
                last.then_inc(done, 1)

            pe.wait_ge(s_wout, 16)
            pe.wait_ge(s_pool, 2 * G)
            pe.wait_ge(s_tailev, 2)

            def pool_half(j):
                if j >= 2:
                    pe.wait_ge(s_halfev, j - 1)
                output(j, 6 - 2 * (j % 2), 0, s_half)

            for j in range(J - 1):
                pool_half(j)
                if j == J - 3:
                    pe.wait_ge(s_glu, G)
                    tails_of(lambda c: glu_p[:, c, CB + SEQ - CB:], CB, 0)
                    pe.wait_ge(s_newest, 2)
                    tails_of(lambda c: newest[1][:, c, :], NS, 1)

            pe.wait_ge(s_diag, 1)
            for n in range(PE_TAPS):
                t = TAPS - PE_TAPS + n
                last = pe.matmul(ps[:, 2, :], lhsT=tap_diag[:, n, :], rhs=glu_p[:, G - 1, t:t + SEQ], start=n == 0, stop=n == PE_TAPS - 1)
            last.then_inc(s_taps, 1)

            LN_BANK = (0, 1, 2, 3, 4)
            pe.wait_ge(s_convp, (TAPS + 1) * G + 1 - PE_TAPS)
            pe.wait_ge(s_convs, 3 * G)
            pe.wait_ge(s_tailev, 4)
            pe.wait_ge(s_halfev, J - 1)
            for j in range(J):
                for c in range(G):
                    last = pe.transpose(ps[0:rows[j], LN_BANK[j], c * P:(c + 1) * P], conv[:, c, j * P:j * P + rows[j]], ident[:])
                last.then_inc(s_lnf, 1)
            pool_half(J - 1)
            for j in range(J):
                r = rows[j]
                pe.wait_ge(s_nrm, j + 1)
                for c in range(G):
                    last = pe.transpose(ps[:, LN_BANK[j], c * P:c * P + r], centred[j][0:r, c * P:(c + 1) * P], ident[0:r, 0:r])
                last.then_inc(s_lnb, 1)

            def conv_half(j):
                pe.wait_ge(s_conv, G * (j + 1))
                if j >= 2:
                    pe.wait_ge(s_h, J + j - 1)
                output(j, 6 - 4 * (j % 2), G, s_op)

            pe.wait_ge(s_halfev, J)

            def logits(j):
                r = rows[j]
                pe.wait_ge(s_hr, j + 1)
                turn(row_buf[j % 2], r, 2 * j - 1 if j else None, s_hnT, s_rt)
                pe.wait_ge(s_hnT, 2 * j + 2)
                if j:
                    pe.wait_ge(s_L, j)
                for k in range(K):
                    last = pe.matmul(ps[0:r, 4, j * E:(j + 1) * E], lhsT=xT[j % 2][:, k, 0:r], rhs=router[:, k, :],
                                     start=k == 0, stop=k == K - 1)
                last.then_inc(s_log, 1)

            pe.wait_ge(s_router, 32)
            pe.wait_ge(s_nrm, J)
            conv_half(0)
            pe.wait_ge(s_conv, G * J)
            conv_half(1)
            pe.wait_ge(s_conv, G * J)
            def rank(j):
                pe.wait_ge(s_mask, j + 1)
                for i in range(j):
                    pe.matmul(ps[:, 5, j * E:(j + 1) * E], lhsT=ones[:], rhs=mask[:, i, :], start=i == 0, stop=False)
                r = rows[j]
                return pe.matmul(ps[:, 5, j * E:(j + 1) * E], lhsT=before[0:r, :], rhs=mask[0:r, j, :], start=j == 0, stop=True)

            for j in range(J):
                logits(j)
                if j + 2 < J:
                    conv_half(j + 2)
                if j >= 1:
                    rank(j - 1)
            pe.wait_ge(s_mask, J)
            for j in range(J):
                r = rows[j]
                last = pe.matmul(ps[0:E, 2, 0:J - 1], lhsT=mask[0:r, j, :], rhs=ones[0:r, 0:J - 1], start=j == 0, stop=j == J - 1)
            last.then_inc(s_count, 1)
            rank(J - 1).then_inc(s_rank, 1)
            pe.wait_ge(s_over, 1)
            pe.matmul(ps[:, 3, 0:E + 1], lhsT=ones[0:E, :], rhs=over_before[:], start=True, stop=True).then_inc(s_prefix, 1)
            for j in range(J):
                r = rows[j]
                pe.wait_ge(s_ab, j + 1)
                for k in range(TOP_K):
                    last = pe.matmul(ps[:, 4, J * E:J * E + COLS], lhsT=inA[0:r, j, k, :], rhs=inB[0:r, j, k, :],
                                     start=j == 0 and k == 0, stop=j == J - 1 and k == TOP_K - 1)
            last.then_inc(s_inv, 1)

            def turn_x(i0, it):
                i, b = i0 + 2 * it, i0 % 2
                pe.wait_ge(s_xg[b], 16 * (i0 // 2 + 1) + 16 * it)
                if i0 >= 2:
                    pe.wait_ge(s_h_lo, i - 1)
                for k in range(K):
                    last = pe.transpose(ps[:, k // HALF, k % HALF * P:(k % HALF + 1) * P], row_buf[b][:, k * P:(k + 1) * P], ident[:])
                last.then_inc(s_txd, 1)

            def turn_h(i0, it):
                i = i0 + 2 * it
                pe.wait_ge(s_hdn, i + 1)
                pe.wait_ge(s_x_lo, i + 2)
                for k in range(KF):
                    last = pe.transpose(ps[:, k // HALF, k % HALF * P:(k % HALF + 1) * P], up_s[:, k * P:(k + 1) * P], ident[:])
                last.then_inc(s_thd, 1)

            def product(banks, hi, lo, whi, wlo, stop):
                for lhs, w in ((hi, whi), (hi, wlo), (lo, whi)):
                    for n in range(banks.shape[1]):
                        last = pe.matmul(banks[:, n, :], lhsT=lhs, rhs=w[:, n * 512:(n + 1) * 512], start=False,
                                         stop=stop and lhs is lo)
                return last

            def gate_up_bias(i0, it):
                i = i0 + 2 * it
                pe.wait_ge(s_sel, i + 1)
                if i0:
                    pe.wait_ge(s_free, i)
                for n in range(4):
                    pe.matmul(ps[:, 4 + n, :], lhsT=sel_cur[i0 % 2][:], rhs=bias[:, n * 512:(n + 1) * 512], start=True, stop=False)

            def gate_up(i0, it):
                i = i0 + 2 * it
                pe.wait_ge(s_x_lo, i + 1)
                for k in range(K):
                    c = gu_chunk(i0) + k
                    pe.wait_ge(s_lo, c + 1 + PER_LOOP * it)
                    last = product(ps[:, 4:8, :], x_hi[:, k, :], x_lo[:, k, :], w_hi[:, c % PARTS, :], w_lo[:, c % PARTS, :], k == K - 1)
                    last.then_inc(s_used if k < K - 1 else s_gu, 1)
                pe.wait_ge(s_gu, i + 1)
                pe.sem_inc(s_used, 1)

            def down(i0, it, last_block=False):
                i, b = i0 + 2 * it, i0 % 2
                pe.wait_ge(s_h_lo, i + 1)
                if i0:
                    pe.wait_ge(s_y, i)
                for n in range(2):
                    last = pe.matmul(ps[:, 2 + n, :], lhsT=sel_cur[b][:], rhs=bias[:, 2 * FF + n * 512:2 * FF + (n + 1) * 512],
                                     start=True, stop=False)
                last.then_inc(s_dsel, 1)
                for k in range(KF):
                    c = dn_chunk(i0, last_block) + k // 2
                    if k % 2 == 0:
                        pe.wait_ge(s_lo, c + 1 + PER_LOOP * it)
                    part_of = slice(k % 2 * D, (k % 2 + 1) * D)
                    last = product(ps[:, 2:4, :], h_hi[:, k, :], h_lo[:, k, :], w_hi[:, c % PARTS, part_of], w_lo[:, c % PARTS, part_of], k == KF - 1)
                    if k % 2:
                        last.then_inc(s_used if k < KF - 1 else s_down, 1)
                pe.wait_ge(s_down, i + 1)
                pe.sem_inc(s_used, 1)

            pe.wait_ge(s_biasp, 3)
            gate_up_bias(0, 0)
            turn_x(0, 0)
            gate_up(0, 0)
            turn_x(1, 0)
            turn_h(0, 0)
            gate_up_bias(1, 0)
            gate_up(1, 0)
            turn_x(2, 0)
            down(0, 0)
            turn_h(1, 0)
            nit = n_loops(pe)
            with pe.Fori(0, nit) as it:
                for u in range(2):
                    gate_up_bias(2 + u, it)
                    gate_up(2 + u, it)
                    turn_x(3 + u, it)
                    down(1 + u, it)
                    turn_h(2 + u, it)
            down(1, nit, last_block=True)


_INS = ["x_prompt", "x_sample", "state_pool", "state_conv", "g_mix", "w_in", "pool_w", "pool_scale", "conv_w", "conv_b",
        "conv_ln_g", "conv_ln_b", "w_out", "g_moe", "w_router", "b_router", "w_gate_up", "b_gate_up", "w_down", "b_down",
        "g_final"]
_OUTS = [(1, 512, 1024), (8, 8, 1024), (1, 1, 15, 512), (1, 1, 30, 512), (1, 8, 15, 512), (1, 8, 30, 512)]


def kernel(**inputs):
    import numpy as _np
    import concourse.bacc as _bacc
    from concourse import mybir as _mybir
    from concourse.bass_utils import run_bass_kernel_spmd as _run

    nc = _bacc.Bacc("TRN2", target_bir_lowering=False, num_devices=1)
    arrays, args = {}, []
    for name in _INS:
        a = _np.ascontiguousarray(inputs[name])
        arrays[f"in_{name}_dram"] = a
        args.append(nc.dram_tensor(f"in_{name}_dram", a.shape, _mybir.dt.from_np(a.dtype), kind="ExternalInput").ap())
    for i, shape in enumerate(_OUTS):
        args.append(nc.dram_tensor(f"out_{i}_dram", shape, _mybir.dt.float32, kind="ExternalOutput").ap())
    args.append(nc.dram_tensor("normed_rows_dram", (576, 1024), _mybir.dt.float32, kind="Internal").ap())
    args.append(nc.dram_tensor("choice_rows_dram", (576 * 4, 1024), _mybir.dt.float32, kind="Internal").ap())
    hybrid_moe_step(nc, *args)
    r = _run(nc, [arrays], core_ids=[0])
    return tuple(r.results[0][f"out_{i}_dram"] for i in range(len(_OUTS)))
```
